# Optimizing a Trainium2 kernel written in Bass

```python
import math
import jax, jax.numpy as jnp
from jax import lax
import numpy as np

D_MODEL = 1024
BATCH = 1
SEQ = 512
DEPTH = 2

M_HEADS = 4
M_HEAD_DIM = 256
M_WIDTH = M_HEADS * M_HEAD_DIM
M_CHUNK = 128
CONV_WIDTH = 5
ATT_SLOTS = 8
ATT_HEAD_DIM = 64
ATT_PATTERNS = ((128, 1), (512, 4), (2048, 16))
N_PATTERNS = 3
ATT_HEADS = ATT_SLOTS * N_PATTERNS
ATT_WIDTH = ATT_HEADS * ATT_HEAD_DIM
ATT_OUT = ATT_SLOTS * ATT_HEAD_DIM
D_FF = -(-8 * D_MODEL // (3 * 256)) * 256
DN_ALPHA = (2 * DEPTH) ** 0.25
DN_BETA = (8 * DEPTH) ** -0.25
LN_EPS = 1e-5
NEG = -1e30
IN_SECTIONS = (2 * M_WIDTH, M_WIDTH, M_WIDTH, 4 * M_HEADS, 3 * ATT_WIDTH, 2 * D_MODEL)
N_IN = sum(IN_SECTIONS)


def layer_norm(x, g=None, b=None):
    xf = x.astype(jnp.float32)
    mu = xf.mean(-1, keepdims=True)
    var = jnp.square(xf - mu).mean(-1, keepdims=True)
    y = (xf - mu) * lax.rsqrt(var + LN_EPS)
    if g is not None:
        y = y * g.astype(jnp.float32) + b.astype(jnp.float32)
    return y.astype(x.dtype)

def alibi_slopes():
    h = np.arange(1, ATT_HEADS + 1, dtype=np.float32)
    s = np.exp2(-8.0 * h / ATT_HEADS).astype(np.float32)
    return jnp.asarray(s.reshape(N_PATTERNS, ATT_SLOTS))

def centred_dwconv(x, w, b):
    k, ch = w.shape
    y = lax.conv_general_dilated(x, w[:, None, :], window_strides=(1,),
                                 padding=((k // 2, k // 2),),
                                 dimension_numbers=('NWC', 'WIO', 'NWC'),
                                 feature_group_count=ch)
    return y + b

def mlstm_scan(q, k, v, i_pre, f_pre):
    B, H, S, dk = q.shape
    dv = v.shape[-1]
    nc = S // M_CHUNK

    def chunks(a):
        return jnp.moveaxis(a.reshape(B, H, nc, M_CHUNK, *a.shape[3:]), 2, 0)

    xs = (chunks(q), chunks(k), chunks(v), chunks(i_pre), chunks(jax.nn.log_sigmoid(f_pre)))
    tri = jnp.tril(jnp.ones((M_CHUNK, M_CHUNK), dtype=bool))

    def step(carry, inp):
        C, n, m = carry
        qc, kc, vc, ic, fc = inp
        b = jnp.cumsum(fc, axis=-1)
        log_d = jnp.where(tri, b[..., :, None] - b[..., None, :] + ic[..., None, :], NEG)
        m_inter = b + m[..., None]
        m_t = jnp.maximum(log_d.max(-1), m_inter)
        w_inter = jnp.exp(m_inter - m_t)
        s = jnp.einsum('bhtd,bhsd->bhts', qc, kc) * jnp.exp(log_d - m_t[..., None])
        num = jnp.einsum('bhts,bhsv->bhtv', s, vc) + w_inter[..., None] * jnp.einsum('bhtd,bhdv->bhtv', qc, C)
        den = s.sum(-1) + w_inter * jnp.einsum('bhtd,bhd->bht', qc, n)
        h = num / jnp.maximum(jnp.abs(den), jnp.exp(-m_t))[..., None]
        b_last = b[..., -1]
        log_w = b_last[..., None] - b + ic
        m_new = jnp.maximum(b_last + m, log_w.max(-1))
        w_state = jnp.exp(log_w - m_new[..., None])
        decay = jnp.exp(b_last + m - m_new)
        C = decay[..., None, None] * C + jnp.einsum('bhs,bhsd,bhsv->bhdv', w_state, kc, vc)
        n = decay[..., None] * n + jnp.einsum('bhs,bhsd->bhd', w_state, kc)
        return (C, n, m_new), h

    init = (jnp.zeros((B, H, dk, dv), jnp.float32), jnp.zeros((B, H, dk), jnp.float32),
            jnp.full((B, H), NEG, jnp.float32))
    _, h = lax.scan(step, init, xs)
    return jnp.moveaxis(h, 0, 2).reshape(B, H, S, dv)

def mlstm_branch(qk, v, o_pre, gate_pre, b_gates, conv_w, conv_b, gn_w):
    B, S, _ = v.shape
    f32 = jnp.float32
    qk = jax.nn.silu(centred_dwconv(qk, conv_w.astype(qk.dtype), conv_b.astype(qk.dtype)))

    def heads(a):
        return a.astype(f32).reshape(B, S, M_HEADS, M_HEAD_DIM).transpose(0, 2, 1, 3)

    q, k = jnp.split(qk, 2, axis=-1)
    q = heads(q) * M_HEAD_DIM ** -0.5
    k = heads(k)
    vh = heads(v)
    g = (gate_pre.astype(f32) + b_gates.astype(f32)).reshape(B, S, 4, M_HEADS).transpose(2, 0, 3, 1)
    i_f, f_f, i_b, f_b = g[0], g[1], g[2], g[3]
    flip = lambda a: jnp.flip(a, axis=2)
    h = mlstm_scan(q, k, vh, i_f, f_f) + flip(mlstm_scan(flip(q), flip(k), flip(vh), flip(i_b), flip(f_b)))
    mu = h.mean(-1, keepdims=True)
    var = jnp.square(h - mu).mean(-1, keepdims=True)
    hn = ((h - mu) * lax.rsqrt(var + LN_EPS)).transpose(0, 2, 1, 3).reshape(B, S, M_WIDTH)
    return (jax.nn.sigmoid(o_pre.astype(f32)) * hn * gn_w.astype(f32)).astype(v.dtype)

def banded_attention(q, k, v, slopes, dil, half):
    B, H, G, n, dh = q.shape
    nb = -(-n // half)
    n_pad = nb * half
    pad0 = ((0, 0),) * 3
    qb = jnp.pad(q, pad0 + ((0, n_pad - n), (0, 0))).reshape(B, H, G, nb, half, dh)

    def kblocks(a):
        ap = jnp.pad(a, pad0 + ((half, n_pad - n + half), (0, 0))).reshape(B, H, G, nb + 2, half, dh)
        return jnp.concatenate([ap[:, :, :, :-2], ap[:, :, :, 1:-1], ap[:, :, :, 2:]], axis=-2)

    kb, vb = kblocks(k), kblocks(v)
    qi = jnp.arange(n_pad).reshape(nb, half)
    kj = (jnp.arange(nb) * half - half)[:, None] + jnp.arange(3 * half)[None, :]
    dist = jnp.abs(qi[:, :, None] - kj[:, None, :])
    valid = (dist <= half) & (kj[:, None, :] >= 0) & (kj[:, None, :] < n)
    bias = -slopes[:, None, None, None] * (dil * dist).astype(jnp.float32)
    s = jnp.einsum('bhgnqd,bhgnkd->bhgnqk', qb, kb) * ATT_HEAD_DIM ** -0.5 + bias[None, :, None]
    s = jnp.where(valid, s, NEG)
    lse = jax.nn.logsumexp(s, axis=-1)
    o = jnp.einsum('bhgnqk,bhgnkd->bhgnqd', jnp.exp(s - lse[..., None]), vb)
    return o.reshape(B, H, G, n_pad, dh)[:, :, :, :n], lse.reshape(B, H, G, n_pad)[:, :, :, :n]

def dilated_attention(qkv, slopes):
    B, S, _ = qkv.shape
    qkv = qkv.astype(jnp.float32).reshape(B, S, 3, N_PATTERNS, ATT_SLOTS, ATT_HEAD_DIM)
    outs, lses = [], []
    for g, (win, dil) in enumerate(ATT_PATTERNS):
        n = S // dil

        def to_res(a):
            return a.reshape(B, n, dil, ATT_SLOTS, ATT_HEAD_DIM).transpose(0, 3, 2, 1, 4)

        o, lse = banded_attention(to_res(qkv[:, :, 0, g]), to_res(qkv[:, :, 1, g]),
                                  to_res(qkv[:, :, 2, g]), slopes[g], dil, win // (2 * dil))
        outs.append(o.transpose(0, 3, 2, 1, 4).reshape(B, S, ATT_SLOTS, ATT_HEAD_DIM))
        lses.append(lse.transpose(0, 3, 2, 1).reshape(B, S, ATT_SLOTS))
    w = jax.nn.softmax(jnp.stack(lses, axis=0), axis=0)
    o = (w[..., None] * jnp.stack(outs, axis=0)).sum(0)
    return o.reshape(B, S, ATT_OUT)

def mixer(u, w_in, b_gates, conv_w, conv_b, gn_w, w_a, w_b, w_out, slopes):
    z = u @ w_in
    idx = np.cumsum(IN_SECTIONS)[:-1].tolist()
    qk_m, v_m, o_m, gate_m, qkv_a, gates_br = jnp.split(z, idx, axis=-1)
    y_a = mlstm_branch(qk_m, v_m, o_m, gate_m, b_gates, conv_w, conv_b, gn_w) @ w_a
    y_b = dilated_attention(qkv_a, slopes).astype(u.dtype) @ w_b
    g_a, g_b = jnp.split(gates_br, 2, axis=-1)
    return (jax.nn.sigmoid(g_a) * y_a + jax.nn.sigmoid(g_b) * y_b) @ w_out

def swiglu(u, w1, w3, w2):
    return (jax.nn.silu(u @ w1) * (u @ w3)) @ w2

def first_inputs(seed: int = 0) -> dict:
    key = jax.random.key(seed)
    ks = jax.random.split(key, 24)

    def nrm(k, shape, scale):
        return jax.random.normal(k, shape, jnp.float32) * scale

    f_bias = jnp.linspace(3.0, 6.0, M_HEADS, dtype=jnp.float32)
    b_gates = jnp.concatenate([
        nrm(ks[3], (DEPTH, M_HEADS), 0.1),
        f_bias + nrm(ks[4], (DEPTH, M_HEADS), 0.1),
        nrm(ks[5], (DEPTH, M_HEADS), 0.1),
        f_bias + nrm(ks[6], (DEPTH, M_HEADS), 0.1)], axis=-1)
    return {
        "x": nrm(ks[0], (BATCH, SEQ, D_MODEL), 1.0),
        "c": nrm(ks[1], (BATCH, D_MODEL), 1.0),
        "w_in": nrm(ks[2], (DEPTH, D_MODEL, N_IN), D_MODEL ** -0.5),
        "b_gates": b_gates,
        "conv_w": nrm(ks[7], (DEPTH, CONV_WIDTH, 2 * M_WIDTH), CONV_WIDTH ** -0.5),
        "conv_b": nrm(ks[8], (DEPTH, 2 * M_WIDTH), 0.02),
        "gn_w": 1.0 + nrm(ks[9], (DEPTH, M_WIDTH), 0.02),
        "w_a": nrm(ks[10], (DEPTH, M_WIDTH, D_MODEL), M_WIDTH ** -0.5),
        "w_b": nrm(ks[11], (DEPTH, ATT_OUT, D_MODEL), ATT_OUT ** -0.5),
        "w_out": nrm(ks[12], (DEPTH, D_MODEL, D_MODEL), DN_BETA * D_MODEL ** -0.5),
        "w_ada": nrm(ks[13], (DEPTH, D_MODEL, 6 * D_MODEL), 0.5 * D_MODEL ** -0.5),
        "b_ada": nrm(ks[14], (DEPTH, 6 * D_MODEL), 0.02),
        "ln1_g": 1.0 + nrm(ks[15], (DEPTH, D_MODEL), 0.02),
        "ln1_b": nrm(ks[16], (DEPTH, D_MODEL), 0.02),
        "w1": nrm(ks[17], (DEPTH, D_MODEL, D_FF), D_MODEL ** -0.5),
        "w3": nrm(ks[18], (DEPTH, D_MODEL, D_FF), D_MODEL ** -0.5),
        "w2": nrm(ks[19], (DEPTH, D_FF, D_MODEL), DN_BETA * D_FF ** -0.5),
        "ln2_g": 1.0 + nrm(ks[20], (DEPTH, D_MODEL), 0.02),
        "ln2_b": nrm(ks[21], (DEPTH, D_MODEL), 0.02),
    }

def first_block(x, c, w_in, b_gates, conv_w, conv_b, gn_w, w_a, w_b, w_out, w_ada, b_ada,
              ln1_g, ln1_b, w1, w3, w2, ln2_g, ln2_b):
    slopes = alibi_slopes()
    c_act = jax.nn.silu(c)
    h = layer_norm(x)
    for l in range(DEPTH):
        ada = (c_act @ w_ada[l] + b_ada[l])[:, None, :]
        sh1, sc1, g1, sh2, sc2, g2 = jnp.split(ada, 6, axis=-1)
        u = h * (1.0 + sc1) + sh1
        y = mixer(u, w_in[l], b_gates[l], conv_w[l], conv_b[l], gn_w[l], w_a[l], w_b[l], w_out[l], slopes)
        h = layer_norm(DN_ALPHA * h + g1 * y, ln1_g[l], ln1_b[l])
        u = h * (1.0 + sc2) + sh2
        y = swiglu(u, w1[l], w3[l], w2[l])
        h = layer_norm(DN_ALPHA * h + g2 * y, ln2_g[l], ln2_b[l])
    return h


HEAD_DIM = 64
EPS = 1e-6
LRU_WIDTH = D_MODEL // 2
LRU_BLOCKS = 8
LRU_BLOCK = LRU_WIDTH // LRU_BLOCKS
LRU_CONV = 4
LRU_C = 8.0
SB_HEADS = 8
SB_WIDTH = SB_HEADS * HEAD_DIM
Q_BLOCK = 128
N_EVEN_SPLITS = 5
SWA_HEADS = D_MODEL // HEAD_DIM
SWA_KV_HEADS = 4
SWA_GROUP = SWA_HEADS // SWA_KV_HEADS
WINDOW = 128
D_FF_2 = 2816
FFN_CONV = 3
N_EVEN = (DEPTH + 1) // 2
N_ODD = DEPTH // 2


def rms_norm(x, g):
    xf = x.astype(jnp.float32)
    y = xf * lax.rsqrt(jnp.mean(xf * xf, axis=-1, keepdims=True) + EPS)
    return (y * g.astype(jnp.float32)).astype(x.dtype)

def causal_dwconv(x, w, b):
    k_width, ch = w.shape
    y = lax.conv_general_dilated(
        x, w[:, None, :].astype(x.dtype), window_strides=(1,),
        padding=[(k_width - 1, 0)], dimension_numbers=("NWC", "WIO", "NWC"),
        feature_group_count=ch)
    return y + b.astype(x.dtype)

def adaln_params(c, w, b):
    m = jax.nn.silu(c) @ w + b
    return [t[:, None, :] for t in jnp.split(m, 6, axis=-1)]

def rg_lru(x, wa, ba, wx, bx, lam):
    bsz, seq, width = x.shape
    xb = x.reshape(bsz, seq, LRU_BLOCKS, LRU_BLOCK)
    r = jax.nn.sigmoid((jnp.einsum("bsnk,nkj->bsnj", xb, wa).reshape(bsz, seq, width) + ba).astype(jnp.float32))
    i = jax.nn.sigmoid((jnp.einsum("bsnk,nkj->bsnj", xb, wx).reshape(bsz, seq, width) + bx).astype(jnp.float32))
    log_a = -LRU_C * r * jax.nn.softplus(-lam.astype(jnp.float32))
    a = jnp.exp(log_a)
    u = jnp.sqrt(-jnp.expm1(2.0 * log_a)) * (i * x.astype(jnp.float32))

    def combine(e1, e2):
        a1, b1 = e1
        a2, b2 = e2
        return a1 * a2, a2 * b1 + b2

    _, h = lax.associative_scan(combine, (a, u), axis=1)
    return h.astype(x.dtype)

def stick_breaking(q, k, v):
    bsz, seq, heads, dh = q.shape
    nb = seq // Q_BLOCK
    scale = 1.0 / np.sqrt(dh)
    qb = q.reshape(bsz, nb, Q_BLOCK, heads, dh).transpose(1, 0, 3, 2, 4)
    kh = k.transpose(0, 2, 1, 3)
    vh = v.transpose(0, 2, 1, 3)
    kpos = jnp.arange(seq)

    def block(args):
        qi, blk = args
        z = jnp.einsum("bhqd,bhkd->bhqk", qi, kh).astype(jnp.float32) * scale
        qpos = blk * Q_BLOCK + jnp.arange(Q_BLOCK)
        mask = kpos[None, :] < qpos[:, None]
        sp = jnp.where(mask, jax.nn.softplus(z), 0.0)
        rev = lax.cumsum(sp, axis=3, reverse=True)
        w = jnp.exp(jnp.where(mask, z - rev, -jnp.inf))
        return jnp.einsum("bhqk,bhkd->bhqd", w.astype(v.dtype), vh)

    out = lax.map(block, (qb, jnp.arange(nb)))
    return out.transpose(1, 0, 3, 2, 4).reshape(bsz, seq, heads * dh)

def swa_sinks(q, k, v, sinks):
    bsz, seq, _, dh = q.shape
    nb = seq // WINDOW
    scale = 1.0 / np.sqrt(dh)
    qb = q.reshape(bsz, nb, WINDOW, SWA_KV_HEADS, SWA_GROUP, dh)

    def banded(t):
        tb = t.reshape(bsz, nb, WINDOW, SWA_KV_HEADS, dh)
        prev = jnp.concatenate([jnp.zeros_like(tb[:, :1]), tb[:, :-1]], axis=1)
        return jnp.concatenate([prev, tb], axis=2)

    kk, vv = banded(k), banded(v)
    s = jnp.einsum("bnqkgd,bnjkd->bnkgqj", qb, kk).astype(jnp.float32) * scale
    i = jnp.arange(WINDOW)[:, None]
    j = jnp.arange(2 * WINDOW)[None, :]
    band = (j > i) & (j <= i + WINDOW)
    blk = jnp.arange(nb)[:, None, None]
    mask = band[None] & ((j >= WINDOW)[None] | (blk > 0))
    s = jnp.where(mask[None, :, None, None], s, -jnp.inf)
    sink = sinks.astype(jnp.float32).reshape(SWA_KV_HEADS, SWA_GROUP)[None, None, :, :, None, None]
    m = jnp.maximum(jnp.max(s, axis=-1, keepdims=True), sink)
    p = jnp.exp(s - m)
    p = p / (jnp.sum(p, axis=-1, keepdims=True) + jnp.exp(sink - m))
    out = jnp.einsum("bnkgqj,bnjkd->bnqkgd", p.astype(v.dtype), vv)
    return out.reshape(bsz, seq, SWA_HEADS * dh)

def conv_ffn(h, w_gate, w_up, conv_w, conv_b, w_down):
    a = causal_dwconv(h @ w_gate, conv_w, conv_b)
    return (jax.nn.silu(a) * (h @ w_up)) @ w_down

def second_inputs(seed: int = 0) -> dict:
    key = jax.random.key(seed)
    ks = iter(jax.random.split(key, 40))

    def nrm(shape, scale):
        return jax.random.normal(next(ks), shape, jnp.float32) * scale

    d = D_MODEL
    u = jax.random.uniform(next(ks), (N_EVEN, LRU_WIDTH), jnp.float32, minval=0.9, maxval=0.999)
    a0 = u ** (1.0 / LRU_C)
    lam = jnp.log(a0) - jnp.log1p(-a0)
    return {
        "x": nrm((BATCH, SEQ, d), 1.0),
        "c": nrm((BATCH, d), 1.0),
        "ada_w": nrm((DEPTH, d, 6 * d), 0.5 * d ** -0.5),
        "ada_b": nrm((DEPTH, 6 * d), 0.02),
        "norm_mix_g": 1.0 + nrm((DEPTH, d), 0.02),
        "norm_ffn_g": 1.0 + nrm((DEPTH, d), 0.02),
        "ev_w_in": nrm((N_EVEN, d, N_EVEN_SPLITS * LRU_WIDTH), d ** -0.5),
        "ev_conv_w": nrm((N_EVEN, LRU_CONV, LRU_WIDTH), LRU_CONV ** -0.5),
        "ev_conv_b": nrm((N_EVEN, LRU_WIDTH), 0.02),
        "ev_wa": nrm((N_EVEN, LRU_BLOCKS, LRU_BLOCK, LRU_BLOCK), LRU_BLOCK ** -0.5),
        "ev_ba": nrm((N_EVEN, LRU_WIDTH), 0.02),
        "ev_wx": nrm((N_EVEN, LRU_BLOCKS, LRU_BLOCK, LRU_BLOCK), LRU_BLOCK ** -0.5),
        "ev_bx": nrm((N_EVEN, LRU_WIDTH), 0.02),
        "ev_lam": lam,
        "ev_qn_g": 1.0 + nrm((N_EVEN, HEAD_DIM), 0.02),
        "ev_kn_g": 1.0 + nrm((N_EVEN, HEAD_DIM), 0.02),
        "ev_w_out": nrm((N_EVEN, LRU_WIDTH + SB_WIDTH, d), (LRU_WIDTH + SB_WIDTH) ** -0.5),
        "od_w_in": nrm((N_ODD, d, (SWA_HEADS + 2 * SWA_KV_HEADS) * HEAD_DIM), d ** -0.5),
        "od_qn_g": 1.0 + nrm((N_ODD, HEAD_DIM), 0.02),
        "od_kn_g": 1.0 + nrm((N_ODD, HEAD_DIM), 0.02),
        "od_sinks": nrm((N_ODD, SWA_HEADS), 1.0),
        "od_w_out": nrm((N_ODD, SWA_HEADS * HEAD_DIM, d), (SWA_HEADS * HEAD_DIM) ** -0.5),
        "ffn_w_gate": nrm((DEPTH, d, D_FF_2), d ** -0.5),
        "ffn_w_up": nrm((DEPTH, d, D_FF_2), d ** -0.5),
        "ffn_conv_w": nrm((DEPTH, FFN_CONV, D_FF_2), FFN_CONV ** -0.5),
        "ffn_conv_b": nrm((DEPTH, D_FF_2), 0.02),
        "ffn_w_down": nrm((DEPTH, D_FF_2, d), D_FF_2 ** -0.5),
    }

def second_block(x, c, ada_w, ada_b, norm_mix_g, norm_ffn_g,
              ev_w_in, ev_conv_w, ev_conv_b, ev_wa, ev_ba, ev_wx, ev_bx, ev_lam,
              ev_qn_g, ev_kn_g, ev_w_out,
              od_w_in, od_qn_g, od_kn_g, od_sinks, od_w_out,
              ffn_w_gate, ffn_w_up, ffn_conv_w, ffn_conv_b, ffn_w_down):
    bsz, seq, _ = x.shape
    for layer in range(DEPTH):
        sh1, sc1, g1, sh2, sc2, g2 = adaln_params(c, ada_w[layer], ada_b[layer])
        h = rms_norm(x, norm_mix_g[layer]) * (1.0 + sc1) + sh1
        if layer % 2 == 0:
            e = layer // 2
            xr, gr, q, k, v = jnp.split(h @ ev_w_in[e], N_EVEN_SPLITS, axis=-1)
            xr = causal_dwconv(xr, ev_conv_w[e], ev_conv_b[e])
            hr = rg_lru(xr, ev_wa[e], ev_ba[e], ev_wx[e], ev_bx[e], ev_lam[e])
            ya = hr * jax.nn.gelu(gr)
            q = rms_norm(q.reshape(bsz, seq, SB_HEADS, HEAD_DIM), ev_qn_g[e])
            k = rms_norm(k.reshape(bsz, seq, SB_HEADS, HEAD_DIM), ev_kn_g[e])
            v = v.reshape(bsz, seq, SB_HEADS, HEAD_DIM)
            yb = stick_breaking(q, k, v)
            mix = jnp.concatenate([ya, yb], axis=-1) @ ev_w_out[e]
        else:
            o = layer // 2
            p = h @ od_w_in[o]
            q_w = SWA_HEADS * HEAD_DIM
            kv_w = SWA_KV_HEADS * HEAD_DIM
            q = rms_norm(p[..., :q_w].reshape(bsz, seq, SWA_HEADS, HEAD_DIM), od_qn_g[o])
            k = rms_norm(p[..., q_w:q_w + kv_w].reshape(bsz, seq, SWA_KV_HEADS, HEAD_DIM), od_kn_g[o])
            v = p[..., q_w + kv_w:].reshape(bsz, seq, SWA_KV_HEADS, HEAD_DIM)
            mix = swa_sinks(q, k, v, od_sinks[o]) @ od_w_out[o]
        x = x + g1 * mix
        h = rms_norm(x, norm_ffn_g[layer]) * (1.0 + sc2) + sh2
        x = x + g2 * conv_ffn(h, ffn_w_gate[layer], ffn_w_up[layer], ffn_conv_w[layer],
                              ffn_conv_b[layer], ffn_w_down[layer])
    return x


def setup_inputs(seed=0):
    out = dict(first_inputs(seed))
    for name, value in second_inputs(seed + 1).items():
        if name != "x":
            out[name + "_2"] = value
    return out


def reference(
    x, c, w_in, b_gates, conv_w, conv_b, gn_w, w_a, w_b, w_out, w_ada, b_ada, ln1_g, ln1_b, w1,
    w3, w2, ln2_g, ln2_b, c_2, ada_w_2, ada_b_2, norm_mix_g_2, norm_ffn_g_2, ev_w_in_2,
    ev_conv_w_2, ev_conv_b_2, ev_wa_2, ev_ba_2, ev_wx_2, ev_bx_2, ev_lam_2, ev_qn_g_2,
    ev_kn_g_2, ev_w_out_2, od_w_in_2, od_qn_g_2, od_kn_g_2, od_sinks_2, od_w_out_2,
    ffn_w_gate_2, ffn_w_up_2, ffn_conv_w_2, ffn_conv_b_2, ffn_w_down_2,
):
    x = first_block(
        x, c, w_in, b_gates, conv_w, conv_b, gn_w, w_a, w_b, w_out, w_ada, b_ada, ln1_g, ln1_b,
        w1, w3, w2, ln2_g, ln2_b,
    )
    return second_block(
        x, c_2, ada_w_2, ada_b_2, norm_mix_g_2, norm_ffn_g_2, ev_w_in_2, ev_conv_w_2,
        ev_conv_b_2, ev_wa_2, ev_ba_2, ev_wx_2, ev_bx_2, ev_lam_2, ev_qn_g_2, ev_kn_g_2,
        ev_w_out_2, od_w_in_2, od_qn_g_2, od_kn_g_2, od_sinks_2, od_w_out_2, ffn_w_gate_2,
        ffn_w_up_2, ffn_conv_w_2, ffn_conv_b_2, ffn_w_down_2,
    )


_drawn_inputs = setup_inputs


def setup_inputs(seed=0):
    import zlib

    import numpy as np

    out = dict(_drawn_inputs(seed))
    spreads = {}
    factors = {'conv_w': 5.983,
     'conv_b': 64.0,
     'gn_w': 8.0,
     'b_ada': 5.513,
     'norm_mix_g_2': 8.0,
     'norm_ffn_g_2': 7.621,
     'ev_conv_b_2': 4.595,
     'ev_ba_2': 8.0,
     'ev_bx_2': 8.0,
     'ev_qn_g_2': 8.0,
     'ev_kn_g_2': 21.799,
     'od_qn_g_2': 24.319,
     'od_kn_g_2': 28.196,
     'od_sinks_2': 64.0,
     'ffn_conv_b_2': 8.0}
    for name, (base, spread) in spreads.items():
        noise = np.random.default_rng([zlib.crc32(name.encode()), seed]).standard_normal(out[name].shape)
        drawn = base * np.exp(spread * noise) if base else spread * noise
        out[name] = __import__('jax').numpy.asarray(drawn.astype(out[name].dtype))
    for name, factor in factors.items():
        out[name] = (out[name] * factor).astype(out[name].dtype)
    return out
```

```python
from collections import deque
from contextlib import ExitStack

import numpy as np
import concourse.bass as bass
from concourse import mybir
from concourse.alu_op_type import AluOpType as ALU

F32 = mybir.dt.float32
F32R = mybir.dt.float32r
ACT = mybir.ActivationFunctionType
AX = mybir.AxisListType

S = 512
D = 1024
NT = D // 128
FF = 2816
FT = FF // 128
ALPHA = float(4 ** 0.25)
LN_EPS = 1e-5
RMS_EPS = 1e-6
NEG = -1e30
SLOPES = [float(np.float32(2.0) ** np.float32(-8.0 * h / 24)) for h in range(1, 25)]
OFF = [0, 512, 896, 1152, 1280]

NRAW, NSPLIT, AHEAD = 5, 4, 3
CH = 1024

KB = 1024
BASE = 16512
ARENA = BASE + 112 * KB

C_ID, C_ONE, C_TRI, C_ND1, C_ND2, C_GI, C_COL = 0, 128, 256, 384, 512, 640, 672
C_SEL = 680
NCONST = C_SEL + 512


def shape_constants():
    c = np.zeros((128, NCONST), np.float32)
    p = np.arange(128)[:, None]
    f = np.arange(128)[None, :]
    c[:, C_ID:C_ID + 128] = p == f
    c[:, C_ONE:C_ONE + 128] = 1.0
    c[:, C_TRI:C_TRI + 128] = p >= f
    d = np.abs(p - f)
    c[:, C_ND1:C_ND1 + 128] = np.where(d <= 64, -4.0 * d, -1e33)
    c[:, C_ND2:C_ND2 + 128] = np.where(d % 4 == 0, -4.0 * d, -1e33)
    for t in range(4):
        for x in range(2):
            c[64 * x:64 * x + 64, C_GI + 8 * t + 2 * t + x] = 1.0 / 64
            c[2 * t + x, C_SEL + 128 * t + 64 * x:C_SEL + 128 * t + 64 * x + 64] = 1.0
    c[:, C_COL] = 1.0 / 1024
    c[:, C_COL + 1] = 1.0 / 256
    c[:, C_COL + 2] = 1.0
    w = np.arange(256)[None, :]
    nd0 = np.zeros((128, 1024), np.float32)
    swa = np.zeros((128, 1024), np.float32)
    for b in range(4):
        key = 128 * b - 64 + w
        dist = np.abs(p + 64 - w)
        ok = (dist <= 64) & (key >= 0) & (key < S)
        nd0[:, 256 * b:256 * b + 256] = np.where(ok, -1.0 * dist, -1e33)
        ok = (w > p) & (w <= p + 128) & ((w >= 128) | (b > 0))
        swa[:, 256 * b:256 * b + 256] = np.where(ok, 0.0, NEG)
    return c, nd0, swa


VECS = [("b_ada", 48, 2), ("conv_w", 80, 2), ("conv_b", 16, 2), ("gn_w", 8, 2),
        ("ln1_g", 8, 2), ("ln1_b", 8, 2), ("ln2_g", 8, 2), ("ln2_b", 8, 2),
        ("c", 8, 1), ("c_2", 8, 1), ("ada_b_2", 48, 2), ("norm_mix_g_2", 8, 2),
        ("norm_ffn_g_2", 8, 2), ("ev_conv_w_2", 16, 1), ("ev_conv_b_2", 4, 1), ("ev_ba_2", 4, 1),
        ("ev_bx_2", 4, 1), ("ev_lam_2", 4, 1), ("ffn_conv_w_2", 66, 2), ("ffn_conv_b_2", 22, 2),
        ("ev_qn_g_2", 1, 1), ("ev_kn_g_2", 1, 1), ("od_qn_g_2", 1, 1), ("od_kn_g_2", 1, 1)]


def vec_plan():
    at, plan = 0, {}
    for name, rows, n in VECS:
        for i in range(n):
            plan[(name, i)] = (at, rows)
            at += rows
    return plan, at


class Null:

    shape = ()

    def __getitem__(self, _):
        return self

    def rearrange(self, *_, **__):
        return self

    def bitcast(self, _):
        return self

    def unsqueeze(self, _):
        return self

    def to_broadcast(self, _):
        return self


class Queues:

    def __init__(self):
        self.q = {e: [] for e in ("pe", "act", "dve", "pool", "sp")}
        self.count = {}
        self.seen = {e: {} for e in self.q}

    def wait(self, eng, *tokens):
        need = {}
        stack = list(tokens)
        while stack:
            t = stack.pop()
            if t is None:
                continue
            if isinstance(t, list):
                stack += t
            else:
                need[t[0]] = max(need.get(t[0], 0), t[1])
        for s, v in need.items():
            if self.seen[eng].get(s, 0) < v:
                self.seen[eng][s] = v
                self.q[eng].append((s, v, None))

    def op(self, eng, fn, *tokens, sem=None, by=1):
        self.wait(eng, *tokens)
        sem = sem or eng
        if by:
            self.count[sem] = self.count.get(sem, 0) + by
        self.q[eng].append((sem, by, fn))
        return (sem, self.count.get(sem, 0))

    def now(self):
        return [(e, self.count[e]) for e in ("pe", "act", "dve", "pool") if self.count.get(e)]


class Ring:

    def __init__(self, tiles, tokens=()):
        self.free = deque((t, list(tokens)) for t in tiles)

    def get(self):
        t, w = self.free.popleft()
        return t, w

    def put(self, t, *tokens):
        self.free.append((t, list(tokens)))


def program(nc, A, out, order):
    dry = order is None
    Q = Queues()
    pe = lambda fn, *w, inc=True: Q.op("pe", fn, *w, by=1 if inc else 0)
    act = lambda fn, *w: Q.op("act", fn, *w)
    dve = lambda fn, *w: Q.op("dve", fn, *w)
    pool = lambda fn, *w: Q.op("pool", fn, *w)
    names = {}

    def dma(fn, sem, *w):
        return Q.op("sp", fn, *w, sem=sem, by=16)

    def at(name, kb, shape, dt=F32, base=ARENA):
        if dry:
            return Null()
        n = names[name] = names.get(name, 0) + 1
        return nc.alloc_sbuf_tensor_at(f"{name}_{n}", list(shape), dt, offset=base + int(kb * KB))

    def ring(name, kb, n, width, dt=F32, tokens=(), base=ARENA):
        step = width * 4 / KB
        return Ring([at(f"{name}{i}", kb + i * step, [128, width], dt, base) for i in range(n)], tokens)

    raws = [at(f"raw{i}", 4 * i, [128, CH], F32, BASE) for i in range(NRAW)]
    his = [at(f"whi{i}", 20 + 4 * i, [128, CH], F32R, BASE) for i in range(NSPLIT)]
    los = [at(f"wlo{i}", 36 + 4 * i, [128, CH], F32R, BASE) for i in range(NSPLIT)]
    H = at("H", 52, [128, NT, S], F32, BASE)
    UH = at("UH", 68, [128, NT, S], F32R, BASE)
    UL = at("UL", 84, [128, NT, S], F32R, BASE)
    CO = at("CO", 100, [128, NCONST], F32, BASE)
    plan, nvec = vec_plan()
    ngrp = -(-nvec // 128)
    cb = 100 + NCONST * 4 / KB
    VT = at("VT", cb, [128, ngrp * 128], F32, BASE)
    cb += ngrp * 0.5
    AD = at("AD", cb, [128, 4, 48], F32, BASE)
    cb += 0.75
    SM = at("SM", cb, [128, 160], F32, BASE)
    cb += 0.625
    ST = at("ST", cb, [128, 3, 2, 4, 8], F32, BASE)
    cb += 0.75
    CL = at("CL", cb, [128, 4, 4, 4], F32, BASE)
    cb += 0.25
    EM = at("EM", cb, [128, 2, 4, 4], F32, BASE)
    cb += 0.125
    assert cb <= 112, cb

    ident = CO[:, C_ID:C_ID + 128]
    ones = CO[:, C_ONE:C_ONE + 128]
    tri = CO[:, C_TRI:C_TRI + 128]
    inv1024 = CO[:, C_COL:C_COL + 1]
    inv256 = CO[:, C_COL + 1:C_COL + 2]
    onec = CO[:, C_COL + 2:C_COL + 3]

    def vec(name, i, j, n=1):
        a = plan[(name, i)][0] + j
        return VT[:, a:a + n]

    PS = Ring([Null()] * 8 if dry else [nc.psum_tensor(f"ps{i}", [128, 512], F32).__enter__() for i in range(8)])

    def mm(o, l, r, start, stop, *w, inc=False, skip=False):
        return pe(lambda e: e.matmul(o, l, r, start=start, stop=stop, skip_group_check=skip), *w, inc=inc)

    def tr(o, i, idn, *w, inc=False):
        return pe(lambda e: e.transpose(o, i, idn), *w, inc=inc)

    def copy(eng, o, i, *w):
        if eng == "act":
            return act(lambda e: e.activation(o, i, ACT.Copy), *w)
        return Q.op(eng, lambda e: e.tensor_copy(o, i), *w)

    def af(o, i, f, *w, **k):
        return act(lambda e: e.activation(o, i, f, **k), *w)

    def tt(o, a, b, op, *w, eng="dve"):
        return Q.op(eng, lambda e: e.tensor_tensor(o, a, b, op), *w)

    def ts(o, a, s1, s2, op0, op1, *w, eng="dve"):
        if s2 is None:
            return Q.op(eng, lambda e: e.tensor_scalar(o, a, s1, None, op0), *w)
        return Q.op(eng, lambda e: e.tensor_scalar(o, a, s1, s2, op0, op1), *w)

    def stt(o, a, s, b, op0, op1, *w):
        return dve(lambda e: e.scalar_tensor_tensor(out=o, in0=a, scalar=s, in1=b, op0=op0, op1=op1), *w)

    def recip(o, i, *w):
        return dve(lambda e: e.reciprocal(o, i), *w)

    used = []
    st = {"get": 0, "load": 0, "split": 0}
    raw_free = [[] for _ in range(NRAW)]
    raw_done = set()
    sp_free = [[] for _ in range(NSPLIT)]
    sp_open = [False] * NSPLIT
    chunk = {}

    def load(i):
        split, name, lay, k0, kn, c0, cw = order[i]
        slot = i % NRAW
        W = A[name][lay]
        src = W[k0 * 128:(k0 + kn) * 128, c0:c0 + cw].rearrange("(t p) n -> p t n", p=128)
        dst = raws[slot][:, 0:kn * cw].rearrange("p (t n) -> p t n", t=kn)
        tok = dma(lambda e: e.dma_start(dst, src), f"w{slot}", raw_free[slot])
        chunk[i] = {"tok": tok, "slot": slot, "n": kn * cw}

    def splitw(i):
        c = chunk[i]
        s = st["split"] % NSPLIT
        assert not sp_open[s]
        st["split"] += 1
        sp_open[s] = True
        n = c["n"]
        raw, hi, lo = raws[c["slot"]], his[s], los[s]
        t1 = copy("act", hi[:, 0:n], raw[:, 0:n], c["tok"], sp_free[s])
        t2 = tt(lo[:, 0:n], raw[:, 0:n], hi[:, 0:n].bitcast(F32), ALU.subtract, t1, sp_free[s], eng="pool")
        raw_free[c["slot"]] = [t2]
        raw_done.add(i)
        c.update(hi=hi, lo=lo, s=s, w1=[t1], w2=[t2])

    st["nsplit"] = 0

    def pump(i):
        j = st["nsplit"]
        while True:
            while st["load"] < len(order) and (st["load"] < NRAW or (st["load"] - NRAW) in raw_done):
                load(st["load"])
                st["load"] += 1
            if j > min(i + AHEAD, len(order) - 1) or j >= st["load"]:
                break
            if order[j][0]:
                if sp_open[st["split"] % NSPLIT]:
                    break
                splitw(j)
            j += 1
        st["nsplit"] = j

    def weights(spec):
        i = st["get"]
        st["get"] += 1
        if dry:
            used.append(spec)
            return {"i": i, "hi": Null(), "lo": Null(), "raw": Null(), "w1": [], "w2": [], "tok": None}
        assert order[i] == spec
        pump(i)
        c = chunk[i]
        c["i"] = i
        if not spec[0]:
            c["raw"] = raws[c["slot"]]
        else:
            assert "hi" in c
        return c

    def weights_done(c, tok):
        if dry:
            return
        if "s" in c:
            sp_open[c["s"]] = False
            sp_free[c["s"]] = [tok]
        else:
            raw_free[c["slot"]] = [tok]
            raw_done.add(c["i"])

    def mm3(o, wh, wl, xh, xl, first, last, wtok, xtok):
        mm(o, wh, xh, first, False, wtok[0], xtok)
        mm(o, wh, xl, False, False)
        return mm(o, wl, xh, False, last, wtok[1], inc=last)

    def lin_tile(name, lay, c0, KT, XH, XL, xtok):
        bank, bw = PS.get()
        for k0 in range(0, KT, 8):
            kn = min(8, KT - k0)
            c = weights((True, name, lay, k0, kn, c0, 128))
            Q.wait("pe", bw)
            for kt in range(kn):
                k = k0 + kt
                last = kt == kn - 1
                mm(bank[:, :], c["hi"][:, kt * 128:(kt + 1) * 128], XH[:, k, :], k == 0, False, c["w1"], xtok[k])
                mm(bank[:, :], c["hi"][:, kt * 128:(kt + 1) * 128], XL[:, k, :], False, False)
                tok = mm(bank[:, :], c["lo"][:, kt * 128:(kt + 1) * 128], XH[:, k, :], False, k == KT - 1,
                         c["w2"], inc=last)
            weights_done(c, tok)
        return bank, tok

    def lin_rows(name, lay, c0, blocks, XH, XL, xtok):
        banks = [PS.get() for _ in blocks]
        for k0 in range(0, NT, 2):
            c = weights((True, name, lay, k0, 2, c0, 512))
            for kt in range(2):
                k = k0 + kt
                for (cols, m), (bank, bw) in zip(blocks, banks):
                    o = bank[0:m, :]
                    wh, wl = (c[x][:, kt * 512:(kt + 1) * 512] for x in ("hi", "lo"))
                    mm(o, XH[:, k, cols], wh, k == 0, False, c["w1"], xtok[k], bw)
                    mm(o, XH[:, k, cols], wl, False, False, c["w2"])
                    tok = mm(o, XL[:, k, cols], wh, False, k == NT - 1, inc=True)
            weights_done(c, tok)
            yield
        return [b for b, _ in banks], tok

    def hilo(hi, lo, src, w, eng="dve"):
        t1 = copy("act", hi, src, w)
        t2 = tt(lo, src, hi.bitcast(F32), ALU.subtract, t1, w, eng=eng)
        return t1, t2

    CS = SM[:, 0:16]
    cs_tok = []

    def ada_units():
        for blk, (wn, cc) in enumerate((("w_ada", 0), ("w_ada", 0), ("ada_w_2", 8), ("ada_w_2", 8))):
            for part in range(3):
                bank, bw = PS.get()
                for m in range(16):
                    c = weights((False, wn, blk % 2, 0, 8, (part * 16 + m) * 128, 128))
                    for kt in range(8):
                        tok = mm(bank[:, m:m + 1], c["raw"][:, kt * 128:(kt + 1) * 128],
                                 CS[:, cc + kt:cc + kt + 1], kt == 0, kt == 7, c["tok"], cs_tok, bw,
                                 inc=kt == 7)
                    weights_done(c, tok)
                    if m < 15:
                        yield
                bn = "b_ada" if blk < 2 else "ada_b_2"
                t = tt(AD[:, blk, part * 16:part * 16 + 16], bank[:, 0:16], vec(bn, blk % 2, part * 16, 16),
                       ALU.add, tok, vt_tok)
                PS.put(bank, t)
                ad_tok[(blk, part)] = t
                yield

    ad_tok = {}
    fill = ada_units()

    def filler(n):
        for _ in range(n):
            if next(fill, 1) == 1:
                break

    def need_ada(blk, part):
        while (blk, part) not in ad_tok:
            next(fill)
        return ad_tok[(blk, part)]

    def ad(blk, j, t=0, n=8):
        return AD[:, blk, 8 * j + t:8 * j + t + n]

    c_tok = dma(lambda e: e.dma_start(CO[:, :], A["const"]), "c0")
    rows = at("rows", 0, [128, ngrp, 128])
    z_tok = pool(lambda e: e.memset(rows[:, :, :], 0.0))
    X0 = at("X0", 8, [128, 4, D])
    x_tok = dma(lambda e: e.dma_start(X0[:, :, :], A["x"][0].rearrange("(b p) d -> p b d", p=128)), "c1")
    v_tok = None
    for name, nr, n in VECS:
        for i in range(n):
            a, _ = plan[(name, i)]
            if nr == 1:
                for x in range(2):
                    v_tok = dma(lambda e, a=a, x=x, name=name: e.dma_start(
                        rows[a % 128:a % 128 + 1, a // 128, 64 * x:64 * x + 64], A[name]), "c2", z_tok)
                continue
            if name in ("c", "c_2", "ev_ba_2", "ev_bx_2", "ev_lam_2"):
                src = A[name].rearrange("a (r p) -> (a r) p", p=128)
            elif name in ("conv_w", "ffn_conv_w_2", "ev_conv_w_2"):
                src = A[name][i].rearrange("a (r p) -> (a r) p", p=128)
            else:
                src = A[name][i].rearrange("(r p) -> r p", p=128)
            r = 0
            while r < nr:
                g, q = divmod(a + r, 128)
                m = min(nr - r, 128 - q)
                v_tok = dma(lambda e, g=g, q=q, m=m, r=r, src=src: e.dma_start(
                    rows[q:q + m, g, :], src[r:r + m, :]), "c2", z_tok)
                r += m
    BG = SM[0:16, 16:18]
    for i in range(2):
        bg_tok = dma(lambda e, i=i: e.dma_start(BG[:, i:i + 1], A["b_gates"][i].rearrange("(a b) -> a b", b=1)), "c3")
    SK = SM[0:1, 20:36]
    sk_tok = dma(lambda e: e.dma_start(SK, A["od_sinks_2"]), "c3")
    vt_tok = []
    for g0 in range(0, ngrp, 4):
        bank, bw = PS.get()
        n = min(4, ngrp - g0)
        for g in range(n):
            tok = tr(bank[:, g * 128:(g + 1) * 128], rows[:, g0 + g, :], ident, c_tok, v_tok, bw, inc=g == n - 1)
        t = copy("dve", VT[:, g0 * 128:(g0 + n) * 128], bank[:, 0:n * 128], tok)
        PS.put(bank, t)
        vt_tok.append(t)
    for i, cn in enumerate(("c", "c_2")):
        cs_tok.append(af(CS[:, 8 * i:8 * i + 8], vec(cn, 0, 0, 8), ACT.Silu, vt_tok))
    SKB = SM[:, 36:52]
    bank, bw = PS.get()
    tok = mm(bank[:, 0:16], CO[0:1, C_ONE:C_ONE + 128], SK, True, True, sk_tok, c_tok, bw, inc=True)
    skb_tok = copy("dve", SKB, bank[:, 0:16], tok)
    PS.put(bank, skb_tok)
    C8 = SM[:, 52:56]
    t = stt(C8, vec("ev_lam_2", 0, 0, 4), -1.0, vec("ev_lam_2", 0, 0, 4), ALU.mult, ALU.min, vt_tok)
    t = af(C8, C8, ACT.Exp, t)
    t = af(C8, C8, ACT.Ln, t, bias=1.0)
    LM = SM[:, 56:60]
    t1 = ts(LM, vec("ev_lam_2", 0, 0, 4), -1.0, 0.0, ALU.mult, ALU.max, vt_tok)
    t = tt(C8, C8, LM, ALU.add, t, t1)
    c8_tok = ts(C8, C8, 8.0, None, ALU.mult, None, t)
    QG = SM[:, 60:64]
    t = None
    for i, (vn, sc) in enumerate((("ev_qn_g_2", 0.125), ("ev_kn_g_2", 1.0), ("od_qn_g_2", 0.125), ("od_kn_g_2", 1.0))):
        qg_tok = ts(QG[:, i:i + 1], vec(vn, 0, 0, 1), sc, None, ALU.mult, None, vt_tok)

    S1, B1, MC, RC, GB = (SM[:, 64 + 8 * i:72 + 8 * i] for i in range(5))
    HM, HR = SM[:, 104:108], SM[:, 108:112]
    MM_, EX, DN = SM[:, 112:116], SM[:, 116:120], SM[:, 120:128]

    ncol = SM[:, 128:136]
    sqt = at("sqt", 24, [128, D])
    lt = []
    for b in range(4):
        xb = X0[:, b, :]
        m = ncol[:, b:b + 1]
        t = dve(lambda e, m=m, xb=xb: e.tensor_reduce(m, xb, AX.X, ALU.add), x_tok)
        t = ts(m, m, 1.0 / D, None, ALU.mult, None, t)
        t = ts(xb, xb, m, None, ALU.subtract, None, t)
        v = ncol[:, 4 + b:5 + b]
        t = af(sqt[:, :], xb, ACT.Square, t, lt, accum_out=v)
        lt = [t]
        t = ts(v, v, 1.0 / D, LN_EPS, ALU.mult, ALU.add, t)
        t = af(v, v, ACT.Sqrt, t)
        t = recip(v, v, t)
        t = ts(xb, xb, v, None, ALU.mult, None, t)
    xn_tok = t

    def norm_tiles():
        w = Q.now()
        return ring("nrm", 88, 2, 512, tokens=w), at("nrd", 92, [128, 4, 128]), w

    def spread(cols, Dt, lhs, w):
        t = tt(Dt[:, :, :], ident.unsqueeze(1).to_broadcast([128, 4, 128]),
               cols.unsqueeze(2).to_broadcast([128, 4, 128]), ALU.mult, w)
        bank, bw = PS.get()
        tok = mm(bank[:, :], lhs, Dt[:, :, :].rearrange("p a b -> p (a b)"), True, True, t, bw, inc=True)
        return bank, tok

    def rstd(cols, src, eps, w):
        t = ts(cols, src, eps, None, ALU.add, None, w)
        t = af(cols, cols, ACT.Sqrt, t)
        return recip(cols, cols, t)

    def colsum(bank, bw, tile, weight, first, *w):
        for b in range(4):
            tok = mm(bank[:, b:b + 1], tile[:, b * 128:(b + 1) * 128], weight, first and b == 0, True, *w, bw,
                     inc=b == 3, skip=True)
        return tok

    def modulated(kt, x, xt, tmp, w):
        t1, t2 = hilo(UH[:, kt, :], UL[:, kt, :], x, xt)
        return [t1, t2]

    def norm_ln(htok, g, b, keep, mod):
        sq, Dt, w0 = norm_tiles()
        bank, bw = PS.get()
        for kt in range(NT):
            tok = colsum(bank, bw, H[:, kt, :], inv1024, kt == 0, htok[kt])
        filler(6)
        t = copy("dve", MC[:, 0:4], bank[:, 0:4], tok, w0)
        PS.put(bank, t)
        if mod:
            blk, jsc, jsh, part = mod
            ta = [need_ada(blk, p) for p in part]
            ta = ts(S1, ad(blk, jsc), 1.0, None, ALU.add, None, ta, w0)
            tb = tt(B1, S1, b, ALU.mult, ta)
            mt = tt(B1, B1, ad(blk, jsh), ALU.add, tb)
        gt = ts(GB, b, keep, None, ALU.mult, None, w0)
        pm, tok = spread(MC[:, 0:4], Dt, ones, t)
        vb, vw = PS.get()
        for kt in range(NT):
            t = tt(H[:, kt, :], H[:, kt, :], pm[:, :], ALU.subtract, tok)
            htok[kt] = t
            s, sw = sq.get()
            t = af(s[:, :], H[:, kt, :], ACT.Square, t, sw)
            vt = colsum(vb, vw, s, inv1024, kt == 0, t)
            sq.put(s, vt)
            filler(1)
        PS.put(pm, htok[-1])
        t = rstd(RC[:, 0:4], vb[:, 0:4], LN_EPS, [vt, w0])
        PS.put(vb, t)
        pr, tok = spread(RC[:, 0:4], Dt, ones, t)
        filler(6)
        ut = []
        for kt in range(NT):
            t = stt(H[:, kt, :], H[:, kt, :], g[:, kt:kt + 1], pr[:, :], ALU.mult, ALU.mult, tok, htok[kt])
            if mod:
                s, sw = sq.get()
                t1 = ts(s[:, :], H[:, kt, :], S1[:, kt:kt + 1], B1[:, kt:kt + 1], ALU.mult, ALU.add, t, mt, sw)
                u = modulated(kt, s[:, :], t1, None, None)
                sq.put(s, *u)
                ut.append(u)
            htok[kt] = [af(H[:, kt, :], H[:, kt, :], ACT.Identity, t, gt, ut[-1:] and ut[-1],
                           scale=keep, bias=GB[:, kt:kt + 1])]
        PS.put(pr, t)
        return ut

    def norm_rms(htok, g, mod):
        sq, Dt, w0 = norm_tiles()
        blk, jsc, jsh, part = mod
        ta = [need_ada(blk, p) for p in part]
        ta = ts(S1, ad(blk, jsc), 1.0, None, ALU.add, None, ta, w0)
        mt = tt(S1, S1, g, ALU.mult, ta)
        vb, vw = PS.get()
        for kt in range(NT):
            s, sw = sq.get()
            t = af(s[:, :], H[:, kt, :], ACT.Square, htok[kt], sw)
            vt = colsum(vb, vw, s, inv1024, kt == 0, t)
            sq.put(s, vt)
            filler(1)
        t = rstd(RC[:, 0:4], vb[:, 0:4], RMS_EPS, [vt, w0])
        PS.put(vb, t)
        pr, tok = spread(RC[:, 0:4], Dt, ones, t)
        filler(6)
        ut = []
        for kt in range(NT):
            s, sw = sq.get()
            t = tt(s[:, :], H[:, kt, :], pr[:, :], ALU.mult, tok, sw, htok[kt])
            t1 = ts(s[:, :], s[:, :], S1[:, kt:kt + 1], ad(blk, jsh, kt, 1), ALU.mult, ALU.add, t, mt)
            u = modulated(kt, s[:, :], t1, None, None)
            sq.put(s, *u)
            ut.append(u)
        PS.put(pr, t)
        return ut

    def residual(name, lay, KT, XH, XL, xtok, htok, gate):
        for m in range(NT):
            bank, tok = lin_tile(name, lay, m * 128, KT, XH, XL, xtok)
            t = stt(H[:, m, :], bank[:, :], gate[:, m:m + 1], H[:, m, :], ALU.mult, ALU.add, tok, htok[m])
            PS.put(bank, t)
            htok[m] = [t]

    def first_attention(lay, ut):
        w0 = Q.now()
        YBH, YBL = at("YBH", 0, [128, 4, S], F32R), at("YBL", 8, [128, 4, S], F32R)
        NUM = at("NUM", 16, [128, 3, 4, S])
        VA = [at(f"VA{i}", 40 + 10 * i, [128, 5, 512]) for i in range(2)]
        vfree = [list(w0), list(w0)]
        qk = ring("qk", 60, 4, 640, tokens=w0)
        sx = ring("sx", 70, 3, 1024, tokens=w0)
        pts = ring("pt", 82, 2, 1024, tokens=w0)
        ND0 = at("ND0", 90, [128, 1024])
        nd_tok = dma(lambda e: e.dma_start(ND0[:, :], A["nd0"]), "c4", w0)
        vtok, made, num_tok = {}, {}, []

        def lins():
            for g in range(3):
                blocks = ([(slice(0, 64), 64)] + [(slice(64 + 128 * i, 192 + 128 * i), 128) for i in range(3)]
                          + [(slice(448, 512), 64)]) if g == 0 else [(slice(q, S, 4), 128) for q in range(4)]
                banks, tok = yield from lin_rows("w_in", lay, 4112 + 3072 + g * 512, blocks, UH, UL, ut)
                vtok[g] = []
                for i, (bank, (_, m)) in enumerate(zip(banks, blocks)):
                    t = copy(("act", "dve")[i % 2], VA[g % 2][0:m, i, :], bank[0:m, :], tok, vfree[g % 2])
                    PS.put(bank, t)
                    vtok[g].append(t)
                for j in range(4):
                    pair = []
                    for which in range(2):
                        yield
                        bank, tok = lin_tile("w_in", lay, 4112 + 1536 * which + g * 512 + j * 128, NT, UH, UL, ut)
                        q, qw = qk.get()
                        if which and g == 0:
                            z1 = pool(lambda e, q=q: e.memset(q[:, 0:64], 0.0), qw)
                            z2 = pool(lambda e, q=q: e.memset(q[:, 576:640], 0.0), qw)
                            t = copy("act", q[:, 64:576], bank[:, :], tok, qw)
                            PS.put(bank, t)
                            t = [t, z1, z2]
                        else:
                            src = bank[:, :] if g == 0 else bank[:, :].rearrange("p (m r) -> p r m", r=4)
                            dst = q[:, 0:512] if g == 0 else q[:, 0:512].rearrange("p (r m) -> p r m", r=4)
                            t = af(dst, src, ACT.Copy, tok, qw, scale=1.0 if which else 0.125)
                            PS.put(bank, t)
                        pair.append((q, t))
                    made[(g, j)] = pair

        def core(g, j):
            (q, qt), (k, kt_) = made[(g, j)]
            pv, pw = PS.get()
            W = 256 if g == 0 else 128
            V = VA[g % 2]
            for x in range(2):
                h = 2 * j + x
                po = 64 * x
                banks = [PS.get() for _ in range(2 if g == 0 else 1)]
                for b in range(4):
                    bank, bw = banks[b * W // 512]
                    c0 = b * W % 512
                    tok = mm(bank[:, c0:c0 + W], q[po:po + 64, b * 128:(b + 1) * 128],
                             k[po:po + 64, b * 128:b * 128 + W], True, True, qt, kt_, bw, inc=True)
                sc, sw = sx.get()
                for i, (bank, _) in enumerate(banks):
                    if g == 0:
                        t = stt(sc[:, 512 * i:512 * i + 512], ND0[:, 512 * i:512 * i + 512], SLOPES[8 * g + h],
                                bank[:, :], ALU.mult, ALU.add, tok, sw, nd_tok)
                    else:
                        a = C_ND1 if g == 1 else C_ND2
                        t = stt(sc[:, 0:512].rearrange("p (b w) -> p b w", b=4),
                                CO[:, a:a + 128].unsqueeze(1).to_broadcast([128, 4, 128]), SLOPES[8 * g + h],
                                bank[:, :].rearrange("p (b w) -> p b w", b=4), ALU.mult, ALU.add, tok, sw)
                    PS.put(bank, t)
                yield
                nm = ST[:, g, 0, :, h]
                t = dve(lambda e, nm=nm, sc=sc: e.tensor_reduce(
                    nm, sc[:, 0:4 * W].rearrange("p (b w) -> p b w", b=4), AX.X, ALU.max, negate=True), t, w0)
                for b in range(4):
                    te = af(sc[:, b * W:(b + 1) * W], sc[:, b * W:(b + 1) * W], ACT.Exp, t,
                            bias=ST[:, g, 0, b, h:h + 1], accum_out=ST[:, g, 1, b, h:h + 1])
                yield
                p, ptw = pts.get()
                jobs = []
                for b in range(4):
                    if g == 0:
                        jobs.append((b, 64, 64, b) if b == 0 else (b, 0, 128, b))
                        jobs.append((b, 128, 64, b + 1) if b == 3 else (b, 128, 128, b + 1))
                    else:
                        jobs.append((b, 0, 128, b))
                et = []
                for i0 in range(0, len(jobs), 4):
                    bank, bw = PS.get()
                    for i in range(i0, i0 + 4):
                        b, c0, m, _ = jobs[i]
                        tok = tr(bank[0:m, (i % 4) * 128:(i % 4 + 1) * 128],
                                 sc[:, b * W + c0:b * W + c0 + m], ident, te, bw, inc=True)
                    if all(jobs[i][2] == 128 for i in range(i0, i0 + 4)):
                        t = [copy(("act", "dve")[(i0 // 4 + x) % 2], p[:, i0 * 128:(i0 + 4) * 128], bank[:, :],
                                  tok, ptw)]
                    else:
                        t = []
                        for i in range(i0, i0 + 4):
                            m = jobs[i][2]
                            t.append(copy(("act", "dve")[(i0 // 4 + x) % 2], p[0:m, i * 128:(i + 1) * 128],
                                          bank[0:m, (i % 4) * 128:(i % 4 + 1) * 128], tok, ptw))
                    PS.put(bank, *t)
                    et += t
                sx.put(sc, tok)
                yield
                for i, (b, c0, m, vb) in enumerate(jobs):
                    last = mm(pv[po:po + 64, b * 128:(b + 1) * 128], V[0:m, vb, h * 64:(h + 1) * 64],
                              p[0:m, i * 128:(i + 1) * 128], g > 0 or i % 2 == 0, g > 0 or i % 2 == 1,
                              et, vtok[g], pw, inc=i == len(jobs) - 1)
                pts.put(p, last)
                yield
            qk.put(q, last)
            qk.put(k, last)
            src = pv[:, :] if g == 0 else pv[:, :].rearrange("p (r m) -> p r m", r=4)
            dst = NUM[:, g, j, :] if g == 0 else NUM[:, g, j, :].rearrange("p (m r) -> p r m", r=4)
            t = copy("act", dst, src, last, w0)
            PS.put(pv, t)
            num_tok.append(t)
            if j == 3:
                vfree[g % 2] = [last]

        L = lins()
        units = [(g, j) for g in range(3) for j in range(4)]
        for n, u in enumerate(units):
            while u not in made:
                next(L, None)
            for _ in core(*u):
                nxt = units[n + 1] if n < 11 else None
                if nxt is None:
                    filler(2)
                elif nxt not in made:
                    next(L, None)
        yt = []

        def tail():
            RR = at("RR", 70, [8, 3, 2, S])
            MI = at("MI", 82, [8, 2, S])
            wr = Q.now()
            rt = {}
            for g in range(3):
                for kd in range(2):
                    bank, bw = PS.get()
                    for b in range(4):
                        tok = tr(bank[0:8, b * 128:(b + 1) * 128], ST[:, g, kd, b, :], ident, wr, bw, inc=b == 3)
                    src = bank[0:8, :] if g == 0 else bank[0:8, :].rearrange("p (r m) -> p r m", r=4)
                    dst = RR[:, g, kd, :] if g == 0 else RR[:, g, kd, :].rearrange("p (m r) -> p r m", r=4)
                    t = copy(("act", "dve")[kd], dst, src, tok, wr)
                    PS.put(bank, t)
                    rt[(g, kd)] = t
            yield
            t = tt(MI[:, 0, :], RR[:, 0, 0, :], RR[:, 1, 0, :], ALU.min, rt[(0, 0)], rt[(1, 0)], wr)
            t = tt(MI[:, 0, :], MI[:, 0, :], RR[:, 2, 0, :], ALU.min, rt[(2, 0)], t)
            te = []
            for g in range(3):
                t1 = tt(RR[:, g, 0, :], MI[:, 0, :], RR[:, g, 0, :], ALU.subtract, t)
                te.append(af(RR[:, g, 0, :], RR[:, g, 0, :], ACT.Exp, t1))
            yield
            p = [tt(RR[:, g, 1, :], RR[:, g, 1, :], RR[:, g, 0, :], ALU.mult, te[g], rt[(g, 1)]) for g in range(3)]
            t = tt(MI[:, 1, :], RR[:, 0, 1, :], RR[:, 1, 1, :], ALU.add, p)
            t = tt(MI[:, 1, :], MI[:, 1, :], RR[:, 2, 1, :], ALU.add, t)
            t = recip(MI[:, 1, :], MI[:, 1, :], t)
            wt = [tt(RR[:, g, 0, :], RR[:, g, 0, :], MI[:, 1, :], ALU.mult, t) for g in range(3)]
            yield
            for j in range(4):
                for g in range(3):
                    bank, bw = PS.get()
                    tok = mm(bank[:, :], CO[0:8, C_SEL + 128 * j:C_SEL + 128 * j + 128], RR[:, g, 0, :],
                             True, True, wt[g], bw, inc=True)
                    t = tt(NUM[:, g, j, :], NUM[:, g, j, :], bank[:, :], ALU.mult, tok, num_tok)
                    PS.put(bank, t)
                t = tt(NUM[:, 0, j, :], NUM[:, 0, j, :], NUM[:, 1, j, :], ALU.add, t)
                t = tt(NUM[:, 0, j, :], NUM[:, 0, j, :], NUM[:, 2, j, :], ALU.add, t)
                yt.append(list(hilo(YBH[:, j, :], YBL[:, j, :], NUM[:, 0, j, :], [t, w0])))
                yield
        return YBH, YBL, yt, tail()

    def first_mlstm(lay, ut, tail):
        w0 = Q.now()
        VM = at("VM", 46, [128, 4, D])
        G4 = at("G4", 62, [4, 4, S])
        Z16 = at("Z16", 90.25, [128, S])
        qk_tiles = [at(f"mq{i}", 70 + 2 * i, [128, S]) for i in range(6)]
        vm_tok = []
        made = {}
        box = {}

        def gates():
            bank, tok = lin_tile("w_in", lay, 4096, NT, UH, UL, ut)
            t = af(Z16[0:16, :], bank[0:16, :], ACT.Identity, tok, bg_tok, w0, bias=BG[:, lay:lay + 1])
            PS.put(bank, t)
            for j in range(4):
                t1 = dma(lambda e, j=j: e.dma_start(G4[:, j, :], Z16[4 * j:4 * j + 4, :]), "c5", t, w0)
            box["g"] = t1
            yield

        def lins():
            for half in range(2):
                banks, tok = yield from lin_rows("w_in", lay, 2048 + 512 * half,
                                                 [(slice(128 * b, 128 * b + 128), 128) for b in range(4)], UH, UL, ut)
                for b, bank in enumerate(banks):
                    t = copy(("act", "dve")[b % 2], VM[:, b, 512 * half:512 * half + 512], bank[:, :], tok, w0)
                    PS.put(bank, t)
                    vm_tok.append(t)
            box["v"] = 1
            yield
            qk, padr, wz = box["qk"], box["pad"], box["w"]
            for h in range(4):
                made[h] = []
                for i, f0 in enumerate((2 * h, 2 * h + 1, 8 + 2 * h, 9 + 2 * h)):
                    bank, tok = lin_tile("w_in", lay, f0 * 128, NT, UH, UL, ut)
                    q, qw = qk.get()
                    pad, pw = padr.get()
                    z = pool(lambda e, pad=pad: e.memset(pad[:, 0:2], 0.0), pw)
                    z2 = pool(lambda e, pad=pad: e.memset(pad[:, 514:516], 0.0), pw)
                    t = copy("act", pad[:, 2:514], bank[:, :], tok, pw)
                    PS.put(bank, t)
                    t = [t, z, z2]
                    t = ts(q[:, :], pad[:, 0:512], vec("conv_w", lay, f0, 1), vec("conv_b", lay, f0, 1),
                           ALU.mult, ALU.add, t, qw)
                    for k in range(1, 5):
                        t = stt(q[:, :], pad[:, k:k + 512], vec("conv_w", lay, 16 * k + f0, 1), q[:, :],
                                ALU.mult, ALU.add, t)
                    padr.put(pad, t)
                    t = af(q[:, :], q[:, :], ACT.Silu, t)
                    made[h].append((q, t))
                    yield

        L = lins()
        for _ in gates():
            pass
        for _ in tail:
            next(L)
        w1 = Q.now()
        YA = at("YA", 16, [128, NT, S])
        RT = at("RT", 32, [4, 4, S])
        ONE = at("ONE", 42, [4, S])
        NR = at("NR", 86.125, [4, 2, S])
        box.update(qk=Ring(qk_tiles, w1), pad=ring("pad", 82, 2, 520, tokens=w1), w=w1)
        o_t = dve(lambda e: e.memset(ONE[:, :], 1.0), w1)
        F4 = G4[:, 1:4:2, :]
        t = stt(RT[:, 0:2, :], F4, -1.0, F4, ALU.mult, ALU.min, box["g"], w1)
        t = af(RT[:, 0:2, :], RT[:, 0:2, :], ACT.Exp, t)
        t = af(RT[:, 0:2, :], RT[:, 0:2, :], ACT.Ln, t, bias=1.0)
        t = stt(RT[:, 2:4, :], F4, 0.0, RT[:, 0:2, :], ALU.min, ALU.subtract, t)

        def scan(o, a, b, init, op0, op1, *w):
            return dve(lambda e: e.tensor_tensor_scan(o, a, b, init, op0, op1), *w)

        rev = [slice(0, S), slice(S - 1, None, -1)]
        fs = [scan(RT[:, d, rev[d]], ONE[:, :], RT[:, 2 + d, rev[d]], 0.0, ALU.mult, ALU.add, t, o_t)
              for d in range(2)]
        at_ = [tt(G4[:, 2 * d, :], G4[:, 2 * d, :], RT[:, d, :], ALU.subtract, fs) for d in range(2)]
        mt = [scan(G4[:, 1 + 2 * d, rev[d]], ONE[:, :], G4[:, 2 * d, rev[d]], NEG, ALU.mult, ALU.max, at_)
              for d in range(2)]
        nt = ts(NR[:, :, :], F4, -1.0, None, ALU.mult, None, mt, w1)
        et = stt(RT[:, 0:2, :], RT[:, 0:2, :], -1.0, F4, ALU.mult, ALU.subtract, mt)
        bank, bw = PS.get()
        for r in range(4):
            src = (G4[:, 0, :], G4[:, 2, :], RT[:, 0, :], RT[:, 1, :])[r]
            for b in range(4):
                tok = tr(bank[:, 16 * r + 4 * b:16 * r + 4 * b + 4], src[:, b * 128:(b + 1) * 128],
                         CO[0:4, 0:4], et, at_, bw, inc=b == 3)
        t = copy("dve", CL[:, :, :, :].rearrange("p a b c -> p (a b c)"), bank[:, 0:64], tok, w1)
        PS.put(bank, t)
        em = af(EM[:, :, :, :], CL[:, 2:4, :, :], ACT.Exp, t, w1)
        while "v" not in box:
            next(L)
        w2 = Q.now()
        PD = [at("PF", 32, [128, 1280]), at("PB", 37, [128, 1280])]
        xr_ = ring("xr", 42, 2, 512, tokens=w2)
        HV = [at(f"HV{i}", 62 + 2 * i, [128, S]) for i in range(2)]
        DT = at("DT", 66, [128, 4, 128])
        SQ = at("SQ", 68, [128, S])
        NA = [at(f"NA{i}", 90.25 + 2 * i, [128, S]) for i in range(2)]
        cl_t = t
        ya_tok = []
        BO = [0, 128, 384, 768]

        def core(h):
            qk = made[h]
            nt_ = []
            wh = Q.now() if h else w2
            for d in range(2):
                bank, bw = PS.get()
                tok = mm(bank[:, :], CO[0:4, h:h + 1].to_broadcast([4, 128]), NR[:, d, :], True, True,
                         nt, bw, inc=True)
                t = copy("act", NA[d][:, :], bank[:, :], tok, wh)
                PS.put(bank, t)
                nt_.append(t)
            ptk = [[], []]
            for sb in range(4):
                bank, bw = PS.get()
                for kt in range(2):
                    tok = mm(bank[:, :], qk[2 + kt][0][:, sb * 128:(sb + 1) * 128], qk[kt][0][:, :], kt == 0, kt == 1,
                             [x[1] for x in qk], bw, inc=kt == 1)
                pt_ = []
                for d in range(2):
                    c0, c1 = (sb * 128, 512) if d == 0 else (0, sb * 128 + 128)
                    n = c1 - c0
                    o = (OFF if d == 0 else BO)[sb]
                    x, xw = xr_.get()
                    t = ts(x[:, 0:n], NA[d][:, c0:c1], CL[:, d, sb, h:h + 1], 0.0, ALU.add, ALU.min,
                           nt_[d], cl_t, xw)
                    t = af(x[:, 0:n], x[:, 0:n], ACT.Exp, t)
                    dg = x[:, 0:128] if d == 0 else x[:, n - 128:n]
                    sg = 1 if d == 0 else -1
                    t = pool(lambda e, dg=dg, sg=sg: e.affine_select(
                        out=dg, in_=dg, compare_op=ALU.is_ge, fill=0.0, base=0, pattern=[[sg, 128]],
                        channel_multiplier=-sg), t)
                    t = stt(PD[d][:, o:o + n], bank[:, c0:c1], 0.0625, x[:, 0:n], ALU.mult, ALU.mult, tok, t, wh)
                    xr_.put(x, t)
                    ptk[d].append(t)
                PS.put(bank, ptk[0][-1], ptk[1][-1])
                if sb % 2:
                    yield
            for x in qk:
                box["qk"].put(x[0], tok)
            dn, dw = PS.get()
            for d in range(2):
                for tb in range(4):
                    sbs = range(0, tb + 1) if d == 0 else range(tb, 4)
                    for i, sb in enumerate(sbs):
                        o = OFF[sb] + (tb - sb) * 128 if d == 0 else BO[sb] + tb * 128
                        tok = mm(dn[:, 4 * d + tb:4 * d + tb + 1], PD[d][:, o:o + 128], onec, i == 0,
                                 i == len(sbs) - 1, ptk, dw, inc=i == len(sbs) - 1)
            t = af(DN, dn[:, 0:8], ACT.Abs, tok, wh)
            PS.put(dn, t)
            t = tt(DN.rearrange("p (d b) -> p d b", d=2), DN.rearrange("p (d b) -> p d b", d=2),
                   EM[:, :, :, h], ALU.max, t, em)
            rt = recip(DN, DN, t)
            nb = {}
            for d in range(2):
                for v in range(2):
                    bank, bw = PS.get()
                    sbs = (0, 1, 2, 3) if d == 0 else (3, 2, 1, 0)
                    for i, sb in enumerate(sbs):
                        c0, c1 = (sb * 128, 512) if d == 0 else (0, sb * 128 + 128)
                        o = (OFF if d == 0 else BO)[sb]
                        tok = mm(bank[:, c0:c1], VM[:, sb, h * 256 + v * 128:h * 256 + v * 128 + 128],
                                 PD[d][:, o:o + c1 - c0], i == 0, i == 3, ptk[d], vm_tok, bw, inc=i == 3)
                    nb[(d, v)] = (bank, tok)
                bk, tk = spread(DN[:, 4 * d:4 * d + 4], DT, ones, [rt, wh] if d == 0 else [rt, nt_])
                t = copy("act", NA[d][:, :], bk[:, :], tk)
                PS.put(bk, t)
                nt_ = [t] if d == 0 else nt_ + [t]
                yield
            hv = []
            for v in range(2):
                b0, t0 = nb[(0, v)]
                b1, t1 = nb[(1, v)]
                x, xw = xr_.get()
                ta = tt(HV[v][:, :], b0[:, :], NA[0][:, :], ALU.mult, t0, nt_, wh)
                tb_ = tt(x[:, :], b1[:, :], NA[1][:, :], ALU.mult, t1, nt_, xw)
                PS.put(b0, ta)
                PS.put(b1, tb_)
                t = tt(HV[v][:, :], HV[v][:, :], x[:, :], ALU.add, ta, tb_)
                xr_.put(x, t)
                hv.append(t)
            bank, bw = PS.get()
            for v in range(2):
                tok = colsum(bank, bw, HV[v], inv256, v == 0, hv[v])
            t = copy("dve", HM, bank[:, 0:4], tok, wh)
            PS.put(bank, t)
            yield
            pm, tok = spread(HM, DT, ones, t)
            bank, bw = PS.get()
            for v in range(2):
                t = tt(HV[v][:, :], HV[v][:, :], pm[:, :], ALU.subtract, tok)
                hv[v] = t
                t = af(SQ[:, :], HV[v][:, :], ACT.Square, t, wh, bank_t if v else None)
                bank_t = colsum(bank, bw, SQ, inv256, v == 0, t)
            PS.put(pm, hv[1])
            yield
            t = rstd(HR, bank[:, 0:4], LN_EPS, [bank_t, wh])
            PS.put(bank, t)
            pr, tok = spread(HR, DT, ones, t)
            for v in range(2):
                t = stt(YA[:, 2 * h + v, :], HV[v][:, :], vec("gn_w", lay, 2 * h + v, 1), pr[:, :],
                        ALU.mult, ALU.mult, tok, w1)
                ya_tok.append(t)
            PS.put(pr, t)

        for h in range(4):
            while len(made.get(h, ())) < 4:
                next(L)
            for _ in core(h):
                if h < 3 and len(made.get(h + 1, ())) < 4 and (dry or len(box["qk"].free)):
                    next(L)
                elif h == 3:
                    filler(3)
        return YA, ya_tok

    def first_block(lay, ut, htok):
        YBH, YBL, ybt, tail = first_attention(lay, ut)
        YA, yat = first_mlstm(lay, ut, tail)
        w0 = Q.now()
        YAH, YAL = at("YAH", 32, [128, NT, S], F32R), at("YAL", 48, [128, NT, S], F32R)
        SH, SL = at("SH", 16, [128, NT, S], F32R), at("SL", 64, [128, NT, S], F32R)
        sg = ring("sg", 80, 6, 512, tokens=w0)
        yt = []
        for m in range(NT):
            bank, tok = lin_tile("w_in", lay, 3072 + 128 * m, NT, UH, UL, ut)
            s, sw = sg.get()
            t = af(s[:, :], bank[:, :], ACT.Sigmoid, tok, sw)
            PS.put(bank, t)
            t = tt(s[:, :], s[:, :], YA[:, m, :], ALU.mult, t, yat)
            u = hilo(YAH[:, m, :], YAL[:, m, :], s[:, :], [t, w0])
            sg.put(s, *u)
            yt.append(list(u))
        w1 = Q.now()
        stk = []
        for m in range(NT):
            r = []
            for which in range(2):
                bank, tok = lin_tile("w_in", lay, 8720 + 1024 * which + 128 * m, NT, UH, UL, ut)
                s, sw = sg.get()
                t = af(s[:, :], bank[:, :], ACT.Sigmoid, tok, sw)
                PS.put(bank, t)
                if which == 0:
                    bank, tok = lin_tile("w_a", lay, 128 * m, NT, YAH, YAL, yt)
                else:
                    bank, tok = lin_tile("w_b", lay, 128 * m, 4, YBH, YBL, ybt)
                t = tt(s[:, :], s[:, :], bank[:, :], ALU.mult, t, tok)
                PS.put(bank, t)
                r.append((s, t))
            t = tt(r[0][0][:, :], r[0][0][:, :], r[1][0][:, :], ALU.add, r[0][1], r[1][1])
            sg.put(r[1][0], t)
            u = hilo(SH[:, m, :], SL[:, m, :], r[0][0][:, :], [t, w1])
            sg.put(r[0][0], *u)
            stk.append(list(u))
        residual("w_out", lay, NT, SH, SL, stk, htok, ad(lay, 2))

    def ffn(lay, ut, htok, blk, conv):
        w0 = Q.now()
        GH, GL = at("GH", 0, [128, FT, S], F32R), at("GL", 44, [128, FT, S], F32R)
        sg = ring("fg", 88, 3, 520, tokens=w0)
        n1, n2, n3 = ("ffn_w_gate_2", "ffn_w_up_2", "ffn_w_down_2") if conv else ("w1", "w3", "w2")
        gt = []
        for m in range(FT):
            bank, tok = lin_tile(n1, lay, 128 * m, NT, UH, UL, ut)
            s, sw = sg.get()
            if conv:
                z = pool(lambda e, s=s: e.memset(s[:, 0:2], 0.0), sw)
                t = copy("act", s[:, 2:514], bank[:, :], tok, sw)
                PS.put(bank, t)
                x, xw = sg.get()
                t = ts(x[:, 0:512], s[:, 0:512], vec("ffn_conv_w_2", lay, m, 1), vec("ffn_conv_b_2", lay, m, 1),
                       ALU.mult, ALU.add, t, z, xw)
                for k in (1, 2):
                    t = stt(x[:, 0:512], s[:, k:k + 512], vec("ffn_conv_w_2", lay, 22 * k + m, 1), x[:, 0:512],
                            ALU.mult, ALU.add, t)
                sg.put(s, t)
                s = x
                t = af(s[:, 0:512], s[:, 0:512], ACT.Silu, t)
            else:
                t = af(s[:, 0:512], bank[:, :], ACT.Silu, tok, sw)
                PS.put(bank, t)
            bank, tok = lin_tile(n2, lay, 128 * m, NT, UH, UL, ut)
            t = tt(s[:, 0:512], s[:, 0:512], bank[:, :], ALU.mult, t, tok)
            PS.put(bank, t)
            u = hilo(GH[:, m, :], GL[:, m, :], s[:, 0:512], [t, w0])
            sg.put(s, *u)
            gt.append(list(u))
        residual(n3, lay, FT, GH, GL, gt, htok, ad(blk, 5))

    def head_norm(tiles, toks, gcol, w0, tmp, RG, sel_n, wr):
        bank, bw = PS.get()
        n = len(tiles)
        for t_, (x, xt) in enumerate(zip(tiles, toks)):
            s, sw = tmp.get()
            t = af(s[:, 0:512], x, ACT.Square, xt, sw)
            tok = mm(bank[0:8, :], CO[:, C_GI + 8 * t_:C_GI + 8 * t_ + 8], s[:, 0:512], t_ == 0, t_ == n - 1,
                     t, bw, inc=True)
            tmp.put(s, tok)
        t = rstd(RG[:, :], bank[0:8, :], RMS_EPS, [tok, wr])
        PS.put(bank, t)
        outs = []
        for t_, (x, xt) in enumerate(zip(tiles, toks)):
            bank, bw = PS.get()
            tok = mm(bank[:, :], CO[0:8, C_SEL + 128 * t_:C_SEL + 128 * t_ + 128], RG[:, :], True, True, t, bw,
                     inc=True)
            t2 = stt(x, x, gcol, bank[:, :], ALU.mult, ALU.mult, tok, xt, qg_tok)
            PS.put(bank, t2)
            outs.append(t2)
        return outs, tok

    def even_layer(ut, htok):
        w0 = Q.now()
        YH, YL = at("YH", 0, [128, NT, S], F32R), at("YL", 16, [128, NT, S], F32R)
        XR, GR = at("XR", 32, [128, 4, S]), at("GR", 40, [128, 4, S])
        QK = at("QK", 48, [128, 8, S])
        V = at("V", 64, [128, 4, 512])
        BD = at("BD", 72, [128, 2, 4, 128])
        RG = [at(f"RG{i}", 76 + 2 * i, [8, S]) for i in range(2)]
        pad = ring("epad", 80, 1, 520, tokens=w0)
        tmp = ring("etmp", 82.125, 6, 512, tokens=w0)
        t = pool(lambda e: e.memset(BD[:, :, :, :], 0.0), w0)
        for a, wn in enumerate(("ev_wa_2", "ev_wx_2")):
            for par in range(2):
                src = A[wn][0].rearrange("(t x) k j -> x k t j", x=2)[par]
                bd_tok = dma(lambda e, a=a, par=par, src=src: e.dma_start(
                    BD[64 * par:64 * par + 64, a, :, 64 * par:64 * par + 64], src), "c6", t)
        yt = [None] * 8
        qt = []
        for i in range(8):
            bank, tok = lin_tile("ev_w_in_2", 0, 1024 + 128 * i, NT, UH, UL, ut)
            t = copy("act", QK[:, i, :], bank[:, :], tok, w0)
            PS.put(bank, t)
            qt.append(t)
        blocks = [(slice(128 * b, 128 * b + 128), 128) for b in range(4)]
        G = lin_rows("ev_w_in_2", 0, 2048, blocks, UH, UL, ut)
        vt = []
        try:
            while True:
                next(G)
        except StopIteration as e:
            banks, tok = e.value
        for b, bank in enumerate(banks):
            t = copy(("act", "dve")[b % 2], V[:, b, :], bank[:, :], tok, w0)
            PS.put(bank, t)
            vt.append(t)
        nq, _ = head_norm([QK[:, i, :] for i in range(4)], qt[0:4], QG[:, 0:1], w0, tmp, RG[0], 8, w0)
        nk, _ = head_norm([QK[:, 4 + i, :] for i in range(4)], qt[4:8], QG[:, 1:2], w0, tmp, RG[1], 8, w0)
        for i in range(4):
            bank, tok = lin_tile("ev_w_in_2", 0, 512 + 128 * i, NT, UH, UL, ut)
            g_t = af(GR[:, i, :], bank[:, :], ACT.Gelu_apprx_tanh, tok, w0)
            PS.put(bank, g_t)
            bank, tok = lin_tile("ev_w_in_2", 0, 128 * i, NT, UH, UL, ut)
            p, pw = pad.get()
            z = pool(lambda e, p=p: e.memset(p[:, 0:3], 0.0), pw)
            t = copy("act", p[:, 3:515], bank[:, :], tok, pw)
            PS.put(bank, t)
            t = ts(XR[:, i, :], p[:, 0:512], vec("ev_conv_w_2", 0, i, 1), vec("ev_conv_b_2", 0, i, 1),
                   ALU.mult, ALU.add, t, z, w0)
            for k in (1, 2, 3):
                t = stt(XR[:, i, :], p[:, k:k + 512], vec("ev_conv_w_2", 0, 4 * k + i, 1), XR[:, i, :],
                        ALU.mult, ALU.add, t)
            pad.put(p, t)
            g = []
            for a, bn in enumerate(("ev_ba_2", "ev_bx_2")):
                bank, bw = PS.get()
                tok = mm(bank[:, :], BD[:, a, i, :], XR[:, i, :], True, True, t, bd_tok, bw, inc=True)
                s, sw = tmp.get()
                t1 = af(s[:, :], bank[:, :], ACT.Sigmoid, tok, sw, bias=vec(bn, 0, i, 1))
                PS.put(bank, t1)
                g.append((s, t1))
            (r, rt), (ii, it) = g
            it = tt(ii[:, :], ii[:, :], XR[:, i, :], ALU.mult, it)
            rt = ts(r[:, :], r[:, :], C8[:, i:i + 1], None, ALU.mult, None, rt, c8_tok)
            th, thw = tmp.get()
            ac, acw = tmp.get()
            t1 = af(th[:, :], r[:, :], ACT.Tanh, rt, thw)
            t2 = af(ac[:, :], r[:, :], ACT.Exp, rt, acw, scale=-1.0)
            t3 = ts(r[:, :], th[:, :], 1.0, None, ALU.add, None, t1, t2)
            t3 = recip(r[:, :], r[:, :], t3)
            t3 = stt(r[:, :], th[:, :], 2.0, r[:, :], ALU.mult, ALU.mult, t3)
            t3 = af(r[:, :], r[:, :], ACT.Sqrt, t3)
            t3 = tt(ii[:, :], ii[:, :], r[:, :], ALU.mult, t3, it)
            t3 = dve(lambda e, th=th, ac=ac, ii=ii: e.tensor_tensor_scan(
                th[:, :], ac[:, :], ii[:, :], 0.0, ALU.mult, ALU.add), t3, t2)
            t3 = tt(th[:, :], th[:, :], GR[:, i, :], ALU.mult, t3, g_t)
            u = hilo(YH[:, i, :], YL[:, i, :], th[:, :], [t3, w0])
            yt[i] = list(u)
            for x in (r, ii, ac):
                tmp.put(x, t3)
            tmp.put(th, *u)
        w1 = Q.now()
        zs = [at(f"zs{i}", 72 + 5 * i, [128, 1280]) for i in range(4)]
        zr = Ring(zs[0:2], w1)
        spr = Ring(zs[2:4], w1)

        def head(h, box):
            i, po = h // 2, 64 * (h % 2)
            z, zw = zr.get()
            sp, spw = spr.get()
            zt = []
            for kb in range(4):
                n = 512 - 128 * kb
                o = OFF[kb]
                bank, bw = PS.get()
                tok = mm(bank[:, 0:n], QK[po:po + 64, 4 + i, kb * 128:(kb + 1) * 128],
                         QK[po:po + 64, i, kb * 128:512], True, True, nq, nk, bw, inc=True)
                t = copy("act", z[:, o:o + n], bank[:, 0:n], tok, zw)
                PS.put(bank, t)
                dg = z[:, o:o + 128]
                zt.append(pool(lambda e, dg=dg: e.affine_select(
                    out=dg, in_=dg, compare_op=ALU.is_gt, fill=NEG, base=0, pattern=[[1, 128]],
                    channel_multiplier=-1), t))
            yield
            t = stt(sp[:, :], z[:, :], -1.0, z[:, :], ALU.mult, ALU.min, zt, spw)
            t = af(sp[:, :], sp[:, :], ACT.Exp, t)
            t = af(sp[:, :], sp[:, :], ACT.Ln, t, bias=1.0)
            t = stt(sp[:, :], z[:, :], 0.0, sp[:, :], ALU.max, ALU.add, t)
            yield
            wt = []
            for kb in range(4):
                n = 512 - 128 * kb
                o = OFF[kb]
                bank, bw = PS.get()
                for k2 in range(kb, 4):
                    tok = mm(bank[:, 128 * (k2 - kb):n], tri if k2 == kb else ones, sp[:, OFF[k2]:OFF[k2 + 1]],
                             k2 == kb, k2 == 3, t, bw, inc=k2 == 3)
                t1 = tt(z[:, o:o + n], z[:, o:o + n], bank[:, 0:n], ALU.subtract, tok)
                PS.put(bank, t1)
                wt.append(af(z[:, o:o + n], z[:, o:o + n], ACT.Exp, t1))
            spr.put(sp, tok)
            yield
            if h % 2 == 0:
                box["pv"] = PS.get()
            pv, pw = box["pv"]
            for kb in range(4):
                tok = mm(pv[po:po + 64, 128 * kb:512], V[:, kb, h * 64:(h + 1) * 64], z[:, OFF[kb]:OFF[kb + 1]],
                         kb == 0, kb == 3, wt, vt, pw, inc=kb == 3)
            zr.put(z, tok)
            if h % 2:
                u = hilo(YH[:, 4 + i, :], YL[:, 4 + i, :], pv[:, :], tok)
                PS.put(pv, *u)
                yt[4 + i] = list(u)
            filler(3)

        box = {}
        live = []
        nxt = 0
        while nxt < 8 or live:
            if nxt < 8 and len(live) < 2 and (not live or live[0][1] >= 2):
                live.append([head(nxt, box), 0])
                nxt += 1
            for g in list(live):
                g[1] += 1
                if next(g[0], "end") == "end":
                    live.remove(g)
        residual("ev_w_out_2", 0, NT, YH, YL, yt, htok, ad(2, 2))

    def odd_layer(ut, htok):
        w0 = Q.now()
        YH, YL = at("OYH", 0, [128, NT, S], F32R), at("OYL", 16, [128, NT, S], F32R)
        QT = at("QT", 32, [128, NT, S])
        KT_ = at("KT", 48, [128, 2, 640])
        V = at("OV", 53, [128, 4, 256])
        MK = at("MK", 57, [128, 1024])
        KD = at("KD", 61, [128, 4, 640])
        sx = ring("ox", 71, 3, 1024, tokens=w0)
        pts = ring("op", 83, 2, 1024, tokens=w0)
        RG = at("ORG", 91, [8, S])
        tmp = ring("otmp", 93, 1, 512, tokens=w0)
        mk_tok = dma(lambda e: e.dma_start(MK[:, :], A["swa"]), "c7", w0)
        kt = []
        for i in range(2):
            bank, tok = lin_tile("od_w_in_2", 0, 1024 + 128 * i, NT, UH, UL, ut)
            z = pool(lambda e, i=i: e.memset(KT_[:, i, 0:128], 0.0), w0)
            t = copy("act", KT_[:, i, 128:640], bank[:, :], tok, w0)
            PS.put(bank, t)
            kt.append([t, z])
        nk, _ = head_norm([KT_[:, i, 128:640] for i in range(2)], kt, QG[:, 3:4], w0, tmp, RG, 4, w0)
        for kv in range(4):
            for x in range(2):
                p0 = 64 * (kv % 2)
                kd_tok = dma(lambda e, kv=kv, x=x, p0=p0: e.dma_start(
                    KD[64 * x:64 * x + 64, kv, :], KT_[p0:p0 + 64, kv // 2, :]), "c8", nk, kt, w0)
        vt = []
        cs = [weights((True, "od_w_in_2", 0, 4 * i, 4, 1280, 256)) for i in range(2)]
        for b in range(4):
            bank, bw = PS.get()
            for k in range(NT):
                c, q = cs[k // 4], k % 4
                xs = slice(128 * b, 128 * b + 128)
                wh, wl = (c[y][:, q * 256:(q + 1) * 256] for y in ("hi", "lo"))
                mm(bank[:, 0:256], UH[:, k, xs], wh, k == 0, False, c["w1"], ut[k], bw)
                mm(bank[:, 0:256], UH[:, k, xs], wl, False, False, c["w2"])
                tok = mm(bank[:, 0:256], UL[:, k, xs], wh, False, k == 7, inc=k == 7)
            t = copy(("act", "dve")[b % 2], V[:, b, :], bank[:, 0:256], tok, w0)
            PS.put(bank, t)
            vt.append(t)
        for c in cs:
            weights_done(c, tok)
        qt = {}

        def qlins():
            for g in range(2):
                toks = []
                for i in range(4 * g, 4 * g + 4):
                    bank, tok = lin_tile("od_w_in_2", 0, 128 * i, NT, UH, UL, ut)
                    t = copy("act", QT[:, i, :], bank[:, :], tok, w0)
                    PS.put(bank, t)
                    toks.append(t)
                    yield
                outs, _ = head_norm([QT[:, i, :] for i in range(4 * g, 4 * g + 4)], toks, QG[:, 2:3], w0, tmp, RG,
                                    8, Q.now())
                for i in range(4):
                    qt[4 * g + i] = outs[i]
                yield

        yt = []

        def pair(i):
            pv, pw = PS.get()
            kv = i // 2
            for x in range(2):
                h, po = 2 * i + x, 64 * x
                banks = [PS.get() for _ in range(2)]
                for b in range(4):
                    bank, bw = banks[b // 2]
                    c0 = 256 * (b % 2)
                    tok = mm(bank[:, c0:c0 + 256], QT[po:po + 64, i, b * 128:(b + 1) * 128],
                             KD[po:po + 64, kv, b * 128:b * 128 + 256], True, True, qt[i], kd_tok, bw, inc=True)
                sc, sw = sx.get()
                for n, (bank, _) in enumerate(banks):
                    t = tt(sc[:, 512 * n:512 * n + 512], bank[:, :], MK[:, 512 * n:512 * n + 512], ALU.add,
                           tok, sw, mk_tok)
                    PS.put(bank, t)
                yield
                wm = Q.now()
                t = dve(lambda e, sc=sc: e.tensor_reduce(
                    MM_, sc[:, :].rearrange("p (b w) -> p b w", b=4), AX.X, ALU.max), t, wm)
                t = ts(MM_, MM_, SKB[:, h:h + 1], -1.0, ALU.max, ALU.mult, t, skb_tok)
                t0 = af(EX, MM_, ACT.Exp, t, wm, bias=SKB[:, h:h + 1])
                for b in range(4):
                    te = af(sc[:, b * 256:(b + 1) * 256], sc[:, b * 256:(b + 1) * 256], ACT.Exp, t,
                            bias=MM_[:, b:b + 1], accum_out=DN[:, b:b + 1])
                t = tt(DN[:, 0:4], DN[:, 0:4], EX, ALU.add, te, t0)
                t = recip(DN[:, 0:4], DN[:, 0:4], t)
                tn = []
                for b in range(4):
                    tn.append(ts(sc[:, b * 256:(b + 1) * 256], sc[:, b * 256:(b + 1) * 256], DN[:, b:b + 1], None,
                                 ALU.mult, None, t))
                yield
                p, ptw = pts.get()
                et = []
                for half in range(2):
                    bank, bw = PS.get()
                    lo_ = 1 if half == 0 else 0
                    for n in range(lo_, 4):
                        c0 = 512 * half + 128 * n
                        tok = tr(bank[:, n * 128:(n + 1) * 128], sc[:, c0:c0 + 128], ident, tn, bw, inc=n == 3)
                    t = copy(("act", "dve")[(half + x) % 2], p[:, 512 * half + 128 * lo_:512 * half + 512],
                             bank[:, 128 * lo_:512], tok, ptw)
                    PS.put(bank, t)
                    et.append(t)
                sx.put(sc, tok)
                yield
                for b in range(4):
                    for n in range(2):
                        if b == 0 and n == 0:
                            continue
                        last = mm(pv[po:po + 64, b * 128:(b + 1) * 128], V[:, b - 1 + n, kv * 64:(kv + 1) * 64],
                                  p[:, 256 * b + 128 * n:256 * b + 128 * n + 128], n == 0 or b == 0, n == 1,
                                  et, vt, pw, inc=b == 3 and n == 1)
                pts.put(p, last)
                yield
            u = hilo(YH[:, i, :], YL[:, i, :], pv[:, :], [last, w0])
            PS.put(pv, *u)
            yt.append(list(u))

        L = qlins()
        for i in range(8):
            while i not in qt:
                next(L)
            for n, _ in enumerate(pair(i)):
                if n % 3 == 0:
                    next(L, None)
                elif i >= 2:
                    filler(1)
        residual("od_w_out_2", 0, NT, YH, YL, yt, htok, ad(3, 2))

    w0 = Q.now()
    sq, Dt, _ = norm_tiles()
    ta = [need_ada(0, 0)]
    ta = ts(S1, ad(0, 1), 1.0, None, ALU.add, None, ta)
    ut, htok = [], []
    for kt in range(NT):
        bank, bw = PS.get()
        for b in range(4):
            tok = tr(bank[:, b * 128:(b + 1) * 128], X0[:, b, kt * 128:(kt + 1) * 128], ident, xn_tok, bw, inc=b == 3)
        s, sw = sq.get()
        t1 = ts(s[:, :], bank[:, :], S1[:, kt:kt + 1], ad(0, 0, kt, 1), ALU.mult, ALU.add, tok, ta, sw)
        ha = af(H[:, kt, :], bank[:, :], ACT.Copy, tok, t1, scale=ALPHA)
        PS.put(bank, t1, ha)
        htok.append([ha])
        u = modulated(kt, s[:, :], t1, None, None)
        sq.put(s, *u)
        ut.append(u)
    for lay in range(2):
        first_block(lay, ut, htok)
        ut = norm_ln(htok, vec("ln1_g", lay, 0, 8), vec("ln1_b", lay, 0, 8), ALPHA, (lay, 4, 3, (1, 2)))
        ffn(lay, ut, htok, lay, False)
        if lay == 0:
            ut = norm_ln(htok, vec("ln2_g", 0, 0, 8), vec("ln2_b", 0, 0, 8), ALPHA, (1, 1, 0, (0,)))
        else:
            norm_ln(htok, vec("ln2_g", 1, 0, 8), vec("ln2_b", 1, 0, 8), 1.0, None)
        need_ada(min(lay + 1, 1), 2)
    for lay in range(2):
        ut = norm_rms(htok, vec("norm_mix_g_2", lay, 0, 8), (2 + lay, 1, 0, (0, 1)))
        (even_layer, odd_layer)[lay](ut, htok)
        ut = norm_rms(htok, vec("norm_ffn_g_2", lay, 0, 8), (2 + lay, 4, 3, (1, 2)))
        ffn(lay, ut, htok, 2 + lay, True)
    w0 = Q.now()
    OT = at("OT", 0, [128, 4, D])
    for b in range(4):
        tt_ = []
        for half in range(2):
            bank, bw = PS.get()
            for i in range(4):
                kt = 4 * half + i
                tok = tr(bank[:, i * 128:(i + 1) * 128], H[:, kt, b * 128:(b + 1) * 128], ident, htok[kt], bw,
                         inc=i == 3)
            t = copy(("act", "dve")[half], OT[:, b, 512 * half:512 * half + 512], bank[:, :], tok, w0)
            PS.put(bank, t)
            tt_.append(t)
        done = dma(lambda e, b=b: e.dma_start(out[0, b * 128:(b + 1) * 128, :], OT[:, b, :]), "out", tt_)
    Q.wait("sp", done)
    if dry:
        return used
    assert st["get"] == len(order)
    emit(nc, Q)


def emit(nc, Q):
    with ExitStack() as ctx:
        sems = {s: ctx.enter_context(nc.semaphore(f"s_{s}")) for s in Q.count}
        block = ctx.enter_context(nc.Block())

        def run(eng, queue):
            for s, n, fn in queue:
                if fn is None:
                    eng.wait_ge(sems[s], n)
                elif n:
                    fn(eng).then_inc(sems[s], n)
                else:
                    fn(eng)

        @block.tensor
        def _(e):
            run(e, Q.q["pe"])

        @block.scalar
        def _(e):
            run(e, Q.q["act"])

        @block.vector
        def _(e):
            run(e, Q.q["dve"])

        @block.gpsimd
        def _(e):
            run(e, Q.q["pool"])

        @block.sync
        def _(e):
            run(e, Q.q["sp"])


_INS = ["x", "c", "w_in", "b_gates", "conv_w", "conv_b", "gn_w", "w_a", "w_b", "w_out", "w_ada", "b_ada",
        "ln1_g", "ln1_b", "w1", "w3", "w2", "ln2_g", "ln2_b", "c_2", "ada_w_2", "ada_b_2", "norm_mix_g_2",
        "norm_ffn_g_2", "ev_w_in_2", "ev_conv_w_2", "ev_conv_b_2", "ev_wa_2", "ev_ba_2", "ev_wx_2", "ev_bx_2",
        "ev_lam_2", "ev_qn_g_2", "ev_kn_g_2", "ev_w_out_2", "od_w_in_2", "od_qn_g_2", "od_kn_g_2", "od_sinks_2",
        "od_w_out_2", "ffn_w_gate_2", "ffn_w_up_2", "ffn_conv_w_2", "ffn_conv_b_2", "ffn_w_down_2"]


def kernel(**inputs):
    import numpy as _np
    import concourse.bacc as _bacc
    from concourse import mybir as _mybir
    from concourse.bass_utils import run_bass_kernel_spmd as _run

    nc = _bacc.Bacc("TRN2", target_bir_lowering=False, num_devices=1)
    arrays, A = {}, {}
    consts = dict(zip(("const", "nd0", "swa"), shape_constants()))
    for name in _INS + list(consts):
        a = consts[name] if name in consts else _np.ascontiguousarray(inputs[name])
        arrays[f"in_{name}"] = a
        A[name] = nc.dram_tensor(f"in_{name}", a.shape, _mybir.dt.from_np(a.dtype), kind="ExternalInput").ap()
    out = nc.dram_tensor("out_0", (1, S, D), _mybir.dt.float32, kind="ExternalOutput").ap()
    order = program(None, A, out, None)
    program(nc, A, out, order)
    r = _run(nc, [arrays], core_ids=[0])
    return r.results[0]["out_0"]
```

```python
from collections import deque
from contextlib import ExitStack

import numpy as np
import concourse.bass as bass
from concourse import mybir
from concourse.alu_op_type import AluOpType as ALU

F32 = mybir.dt.float32
F32R = mybir.dt.float32r
ACT = mybir.ActivationFunctionType
AX = mybir.AxisListType

S = 512
D = 1024
NT = D // 128
FF = 2816
FT = FF // 128
ALPHA = float(4 ** 0.25)
LN_EPS = 1e-5
RMS_EPS = 1e-6
NEG = -1e30
SLOPES = [float(np.float32(2.0) ** np.float32(-8.0 * h / 24)) for h in range(1, 25)]
OFF = [0, 512, 896, 1152, 1280]

NRAW, NSPLIT, AHEAD = 5, 4, 3
CH = 1024

BESIDE = {"w1", "w3", "w2", "ffn_w_gate_2", "ffn_w_up_2", "ffn_w_down_2", "w_a", "w_b", "w_out"}

KB = 1024
BASE = 16512
ARENA = BASE + 112 * KB + 256

C_ID, C_ONE, C_TRI, C_ND1, C_ND2, C_GI = 0, 128, 256, 384, 512, 640
C_SEL = 672
NCONST = C_SEL + 512


def shape_constants():
    c = np.zeros((128, NCONST), np.float32)
    p = np.arange(128)[:, None]
    f = np.arange(128)[None, :]
    c[:, C_ID:C_ID + 128] = p == f
    c[:, C_ONE:C_ONE + 128] = 1.0
    c[:, C_TRI:C_TRI + 128] = p >= f
    d = np.abs(p - f)
    c[:, C_ND1:C_ND1 + 128] = np.where(d <= 64, -4.0 * d, -1e33)
    c[:, C_ND2:C_ND2 + 128] = np.where(d % 4 == 0, -4.0 * d, -1e33)
    for t in range(4):
        for x in range(2):
            c[64 * x:64 * x + 64, C_GI + 8 * t + 2 * t + x] = 1.0 / 64
            c[2 * t + x, C_SEL + 128 * t + 64 * x:C_SEL + 128 * t + 64 * x + 64] = 1.0
    w = np.arange(256)[None, :]
    nd0 = np.zeros((128, 1024), np.float32)
    swa = np.zeros((128, 1024), np.float32)
    for b in range(4):
        key = 128 * b - 64 + w
        dist = np.abs(p + 64 - w)
        ok = (dist <= 64) & (key >= 0) & (key < S)
        nd0[:, 256 * b:256 * b + 256] = np.where(ok, -1.0 * dist, -1e33)
        ok = (w > p) & (w <= p + 128) & ((w >= 128) | (b > 0))
        swa[:, 256 * b:256 * b + 256] = np.where(ok, 0.0, NEG)
    return c, nd0, swa


VECS = [("c", 8, 1), ("c_2", 8, 1), ("b_ada", 48, 2), ("conv_w", 80, 2), ("conv_b", 16, 2), ("gn_w", 8, 2),
        ("ln1_g", 8, 2), ("ln1_b", 8, 2), ("ln2_g", 8, 2), ("ln2_b", 8, 2),
        ("ada_b_2", 48, 2), ("norm_mix_g_2", 8, 2),
        ("norm_ffn_g_2", 8, 2), ("ev_conv_w_2", 16, 1), ("ev_conv_b_2", 4, 1), ("ev_ba_2", 4, 1),
        ("ev_bx_2", 4, 1), ("ev_lam_2", 4, 1), ("ffn_conv_w_2", 66, 2), ("ffn_conv_b_2", 22, 2),
        ("ev_qn_g_2", 1, 1), ("ev_kn_g_2", 1, 1), ("od_qn_g_2", 1, 1), ("od_kn_g_2", 1, 1)]


def vec_plan():
    at, plan = 0, {}
    for name, rows, n in VECS:
        if name == "conv_w":
            at = 128
        for i in range(n):
            plan[(name, i)] = (at, rows)
            at += rows
    return plan, at


class Null:

    shape = ()

    def __getitem__(self, _):
        return self

    def rearrange(self, *_, **__):
        return self

    def bitcast(self, _):
        return self

    def unsqueeze(self, _):
        return self

    def to_broadcast(self, _):
        return self


class Queues:

    def __init__(self):
        self.q = {e: [] for e in ("pe", "act", "dve", "pool", "sp")}
        self.count = {}
        self.seen = {e: {} for e in self.q}

    def wait(self, eng, *tokens):
        need = {}
        stack = list(tokens)
        while stack:
            t = stack.pop()
            if t is None:
                continue
            if isinstance(t, list):
                stack += t
            else:
                need[t[0]] = max(need.get(t[0], 0), t[1])
        for s, v in need.items():
            if self.seen[eng].get(s, 0) < v:
                self.seen[eng][s] = v
                self.q[eng].append((s, v, None))

    def op(self, eng, fn, *tokens, sem=None, by=1):
        self.wait(eng, *tokens)
        sem = sem or eng
        if by:
            self.count[sem] = self.count.get(sem, 0) + by
        self.q[eng].append((sem, by, fn))
        return (sem, self.count.get(sem, 0))

    def now(self):
        return [(e, self.count[e]) for e in ("pe", "act", "dve", "pool") if self.count.get(e)]


class Ring:

    def __init__(self, tiles, tokens=()):
        self.free = deque((t, list(tokens)) for t in tiles)

    def get(self):
        t, w = self.free.popleft()
        return t, w

    def put(self, t, *tokens):
        self.free.append((t, list(tokens)))


def program(nc, A, out, order):
    dry = order is None
    Q = Queues()
    pe = lambda fn, *w, inc=True: Q.op("pe", fn, *w, by=1 if inc else 0)
    act = lambda fn, *w: Q.op("act", fn, *w)
    dve = lambda fn, *w: Q.op("dve", fn, *w)
    pool = lambda fn, *w: Q.op("pool", fn, *w)
    names = {}

    def dma(fn, sem, *w):
        return Q.op("sp", fn, *w, sem=sem, by=16)

    def at(name, kb, shape, dt=F32, base=ARENA):
        if dry:
            return Null()
        n = names[name] = names.get(name, 0) + 1
        return nc.alloc_sbuf_tensor_at(f"{name}_{n}", list(shape), dt, offset=base + int(kb * KB))

    def ring(name, kb, n, width, dt=F32, tokens=(), base=ARENA):
        step = width * 4 / KB
        return Ring([at(f"{name}{i}", kb + i * step, [128, width], dt, base) for i in range(n)], tokens)

    raws = [at(f"raw{i}", 4 * i, [128, CH], F32, BASE) for i in range(NRAW)]
    his = [at(f"whi{i}", 20 + 4 * i, [128, CH], F32R, BASE) for i in range(NSPLIT)]
    los = [at(f"wlo{i}", 36 + 4 * i, [128, CH], F32R, BASE) for i in range(NSPLIT)]
    H = at("H", 52, [128, NT, S], F32, BASE)
    UH = at("UH", 68, [128, NT, S], F32R, BASE)
    UL = at("UL", 84, [128, NT, S], F32R, BASE)
    CO = at("CO", 100, [128, NCONST], F32, BASE)
    plan, nvec = vec_plan()
    ngrp = -(-nvec // 128)
    cb = 100 + NCONST * 4 / KB
    VT = at("VT", cb, [128, ngrp * 128], F32, BASE)
    cb += ngrp * 0.5
    AD = at("AD", cb, [128, 4, 48], F32, BASE)
    cb += 0.75
    SM = at("SM", cb, [128, 160], F32, BASE)
    cb += 0.625
    ST = at("ST", cb, [128, 3, 2, 4, 8], F32, BASE)
    cb += 0.75
    CL = at("CL", cb, [128, 4, 4, 4], F32, BASE)
    cb += 0.25
    EM = at("EM", cb, [128, 2, 4, 4], F32, BASE)
    cb += 0.125
    ACC = at("ACC", cb, [128, 512], F32, BASE)
    assert cb + 2 <= 112.25, cb

    ident = CO[:, C_ID:C_ID + 128]
    ones = CO[:, C_ONE:C_ONE + 128]
    tri = CO[:, C_TRI:C_TRI + 128]
    onec = CO[:, C_ONE:C_ONE + 1]

    def vec(name, i, j, n=1):
        a = plan[(name, i)][0] + j
        return VT[:, a:a + n]

    PS = Ring([Null()] * 8 if dry else [nc.psum_tensor(f"ps{i}", [128, 512], F32).__enter__() for i in range(8)])

    def mm(o, l, r, start, stop, *w, inc=False, skip=False):
        return pe(lambda e: e.matmul(o, l, r, start=start, stop=stop, skip_group_check=skip), *w, inc=inc)

    def tr(o, i, idn, *w, inc=False):
        return pe(lambda e: e.transpose(o, i, idn), *w, inc=inc)

    def copy(eng, o, i, *w):
        if eng == "act":
            return act(lambda e: e.activation(o, i, ACT.Copy), *w)
        return Q.op(eng, lambda e: e.tensor_copy(o, i), *w)

    def af(o, i, f, *w, **k):
        return act(lambda e: e.activation(o, i, f, **k), *w)

    def tt(o, a, b, op, *w, eng="dve"):
        return Q.op(eng, lambda e: e.tensor_tensor(o, a, b, op), *w)

    def ts(o, a, s1, s2, op0, op1, *w, eng="dve"):
        if s2 is None:
            return Q.op(eng, lambda e: e.tensor_scalar(o, a, s1, None, op0), *w)
        return Q.op(eng, lambda e: e.tensor_scalar(o, a, s1, s2, op0, op1), *w)

    def stt(o, a, s, b, op0, op1, *w):
        return dve(lambda e: e.scalar_tensor_tensor(out=o, in0=a, scalar=s, in1=b, op0=op0, op1=op1), *w)

    def recip(o, i, *w):
        return dve(lambda e: e.reciprocal(o, i), *w)

    used = []
    st = {"get": 0, "load": 0, "split": 0, "tiles": 0}
    raw_free = [[] for _ in range(NRAW)]
    raw_done = set()
    sp_free = [[] for _ in range(NSPLIT)]
    sp_open = [False] * NSPLIT
    chunk = {}

    def load(i):
        split, name, lay, k0, kn, c0, cw = order[i]
        slot = i % NRAW
        W = A[name][lay]
        src = W[k0 * 128:(k0 + kn) * 128, c0:c0 + cw].rearrange("(t p) n -> p t n", p=128)
        dst = raws[slot][:, 0:kn * cw].rearrange("p (t n) -> p t n", t=kn)
        tok = dma(lambda e: e.dma_start(dst, src), f"w{slot}", raw_free[slot])
        chunk[i] = {"tok": tok, "slot": slot, "n": kn * cw}

    def splitw(i):
        c = chunk[i]
        s = st["split"] % NSPLIT
        assert not sp_open[s]
        st["split"] += 1
        sp_open[s] = True
        n = c["n"]
        raw, hi, lo = raws[c["slot"]], his[s], los[s]
        t1 = copy("act", hi[:, 0:n], raw[:, 0:n], c["tok"], sp_free[s])
        t2 = tt(lo[:, 0:n], raw[:, 0:n], hi[:, 0:n].bitcast(F32), ALU.subtract, t1, sp_free[s], eng="pool")
        raw_free[c["slot"]] = [t2]
        raw_done.add(i)
        c.update(hi=hi, lo=lo, s=s, w1=[t1], w2=[t2])

    st["nsplit"] = 0

    def pump(i):
        j = st["nsplit"]
        while True:
            while st["load"] < len(order) and (st["load"] < NRAW or (st["load"] - NRAW) in raw_done):
                load(st["load"])
                st["load"] += 1
            if j > min(i + AHEAD, len(order) - 1) or j >= st["load"]:
                break
            if order[j][0]:
                if sp_open[st["split"] % NSPLIT]:
                    break
                splitw(j)
            j += 1
        st["nsplit"] = j

    def weights(spec):
        i = st["get"]
        st["get"] += 1
        if dry:
            used.append(spec)
            return {"i": i, "hi": Null(), "lo": Null(), "raw": Null(), "w1": [], "w2": [], "tok": None}
        assert order[i] == spec
        pump(i)
        c = chunk[i]
        c["i"] = i
        if not spec[0]:
            c["raw"] = raws[c["slot"]]
        else:
            assert "hi" in c
        return c

    def weights_done(c, tok):
        if dry:
            return
        if "s" in c:
            sp_open[c["s"]] = False
            sp_free[c["s"]] = [tok]
        else:
            raw_free[c["slot"]] = [tok]
            raw_done.add(c["i"])

    deferred = deque()

    def run_deferred(n):
        while deferred and n:
            deferred.popleft()()
            n -= 1

    def lin_tiles(tiles, KT, XH, XL, xtok):
        st["tiles"] += 1
        if tiles[0][0] in BESIDE or st["tiles"] % 3 == 0:
            filler(1)
        banks = [PS.get() for _ in tiles]
        toks = [None] * len(tiles)
        for k0 in range(0, KT, 8):
            kn = min(8, KT - k0)
            cs = [weights((True, name, lay, k0, kn, c0, 128)) for name, lay, c0 in tiles]
            for kt in range(kn):
                k = k0 + kt
                for i, (c, (bank, bw)) in enumerate(zip(cs, banks)):
                    wh, wl = (c[x][:, kt * 128:(kt + 1) * 128] for x in ("hi", "lo"))
                    mm(bank[:, :], wh, XH[:, k, :], k == 0, False, c["w1"], xtok[k][0], bw)
                    mm(bank[:, :], wl, XH[:, k, :], False, False, c["w2"])
                    toks[i] = mm(bank[:, :], wh, XL[:, k, :], False, k == KT - 1, xtok[k][1], inc=kt == kn - 1)
            for c, tok in zip(cs, toks):
                weights_done(c, tok)
        run_deferred(1)
        return [(bank, tok) for (bank, _), tok in zip(banks, toks)]

    def lin_tile(name, lay, c0, KT, XH, XL, xtok):
        return lin_tiles([(name, lay, c0)], KT, XH, XL, xtok)[0]

    def lin_rows(name, lay, c0, blocks, XH, XL, xtok):
        banks = [PS.get() for _ in blocks]
        for k0 in range(0, NT, 2):
            c = weights((True, name, lay, k0, 2, c0, 512))
            for kt in range(2):
                k = k0 + kt
                for (cols, m), (bank, bw) in zip(blocks, banks):
                    o = bank[0:m, :]
                    wh, wl = (c[x][:, kt * 512:(kt + 1) * 512] for x in ("hi", "lo"))
                    mm(o, XH[:, k, cols], wh, k == 0, False, c["w1"], xtok[k], bw)
                    mm(o, XH[:, k, cols], wl, False, False, c["w2"])
                    tok = mm(o, XL[:, k, cols], wh, False, k == NT - 1, inc=True)
            weights_done(c, tok)
            run_deferred(1)
            yield
        return [b for b, _ in banks], tok

    def hilo(hi, lo, src, w, eng="dve"):
        t1 = copy("act", hi, src, w)
        t2 = tt(lo, src, hi.bitcast(F32), ALU.subtract, t1, w, eng=eng)
        return t1, t2

    CS = SM[:, 0:16]
    cs_tok = []

    def ada_units():
        free = []
        for blk, (wn, cc) in enumerate((("w_ada", 0), ("w_ada", 0), ("ada_w_2", 8), ("ada_w_2", 8))):
            bn = "b_ada" if blk < 2 else "ada_b_2"
            for q in range(12):
                t = [vt0_tok, cs_tok, free]
                for k0 in range(0, 8, 2):
                    c = weights((False, wn, blk % 2, k0, 2, 512 * q, 512))
                    for kt in range(2):
                        w, k = c["raw"][:, kt * 512:(kt + 1) * 512], CS[:, cc + k0 + kt:cc + k0 + kt + 1]
                        if k0 + kt == 0:
                            t = ts(ACC[:, :], w, k, None, ALU.mult, None, c["tok"], t)
                        else:
                            t = stt(ACC[:, :], w, k, ACC[:, :], ALU.mult, ALU.add, c["tok"], t)
                    weights_done(c, t)
                    yield
                yield
                bank, bw = PS.get()
                for m in range(4):
                    tok = mm(bank[:, m:m + 1], ACC[:, m * 128:(m + 1) * 128], onec, True, True, t, bw, inc=m == 3)
                free = [tok]
                t = tt(AD[:, blk, 4 * q:4 * q + 4], bank[:, 0:4], vec(bn, blk % 2, 4 * q, 4), ALU.add, tok,
                       vt0_tok if blk < 2 else vt_tok)
                PS.put(bank, t)
                ad_tok[(blk, q // 4)] = t
                if q % 4 == 3:
                    ad_done.add((blk, q // 4))
                yield

    ad_done = set()
    ad_tok = {}
    fill = ada_units()

    def filler(n):
        for _ in range(n):
            if next(fill, 1) == 1:
                break

    def need_ada(blk, part):
        while (blk, part) not in ad_done:
            next(fill)
        return ad_tok[(blk, part)]

    def ad(blk, j, t=0, n=8):
        return AD[:, blk, 8 * j + t:8 * j + t + n]

    rows = at("rows", 0, [128, ngrp, 128])
    z_tok = pool(lambda e: e.memset(rows[:, :, :], 0.0))
    X0 = at("X0", 8, [128, 4, D])
    def load_vectors(names, sem):
        for name, nr, n in names:
            for i in range(n):
                a, _ = plan[(name, i)]
                if nr == 1:
                    for x in range(2):
                        v_tok = dma(lambda e, a=a, x=x, name=name: e.dma_start(
                            rows[a % 128:a % 128 + 1, a // 128, 64 * x:64 * x + 64], A[name]), sem, z_tok)
                    continue
                if name in ("c", "c_2", "ev_ba_2", "ev_bx_2", "ev_lam_2"):
                    src = A[name].rearrange("a (r p) -> (a r) p", p=128)
                elif name in ("conv_w", "ffn_conv_w_2", "ev_conv_w_2"):
                    src = A[name][i].rearrange("a (r p) -> (a r) p", p=128)
                else:
                    src = A[name][i].rearrange("(r p) -> r p", p=128)
                r = 0
                while r < nr:
                    g, q = divmod(a + r, 128)
                    m = min(nr - r, 128 - q)
                    v_tok = dma(lambda e, g=g, q=q, m=m, r=r, src=src: e.dma_start(
                        rows[q:q + m, g, :], src[r:r + m, :]), sem, z_tok)
                    r += m
        return v_tok

    BG = SM[0:16, 16:18]
    SK = SM[0:1, 20:36]
    bg_tok, skb_tok, c8_tok, qg_tok = [], [], [], []
    v0_tok = load_vectors(VECS[:3], "c9")
    c_tok = dma(lambda e: e.dma_start(CO[:, :], A["const"]), "c0")
    if not dry:
        pump(-AHEAD - 1)
    x_tok = dma(lambda e: e.dma_start(X0[:, :, :], A["x"][0].rearrange("(b p) d -> p b d", p=128)), "c1")
    vt_tok = []
    S1, B1, GB = (SM[:, 64 + 8 * i:72 + 8 * i] for i in range(3))
    EPS_LN, EPS_RMS, WARM = SM[:, 104:105], SM[:, 105:106], SM[:, 106:107]
    DN = SM[:, 120:128]

    def turn(g0, n, w):
        bank, bw = PS.get()
        for g in range(n):
            tok = tr(bank[:, g * 128:(g + 1) * 128], rows[:, g0 + g, :], ident, c_tok, w, bw, inc=g == n - 1)
        t = copy("dve", VT[:, g0 * 128:(g0 + n) * 128], bank[:, 0:n * 128], tok)
        PS.put(bank, t)
        return t

    def first_norm():
        ncol = SM[:, 128:136]
        sqt = at("sqt", 24, [128, D])
        lt = []
        for b in range(4):
            xb = X0[:, b, :]
            m = ncol[:, b:b + 1]
            t = dve(lambda e, m=m, xb=xb: e.tensor_reduce(m, xb, AX.X, ALU.add), x_tok)
            t = ts(m, m, 1.0 / D, None, ALU.mult, None, t)
            t = ts(xb, xb, m, None, ALU.subtract, None, t)
            v = ncol[:, 4 + b:5 + b]
            t = af(sqt[:, :], xb, ACT.Square, t, lt, accum_out=v)
            lt = [t]
            yield
            t = ts(v, v, 1.0 / D, LN_EPS, ALU.mult, ALU.add, t)
            t = af(v, v, ACT.Sqrt, t)
            yield
            t = recip(v, v, t)
            t = ts(xb, xb, v, None, ALU.mult, None, t)
            xn_tok.append(t)
            yield

    vt0_tok = turn(0, 1, v0_tok)
    for i, cn in enumerate(("c", "c_2")):
        cs_tok.append(af(CS[:, 8 * i:8 * i + 8], vec(cn, 0, 0, 8), ACT.Silu, vt0_tok))
    eps_tok = [dve(lambda e: e.memset(EPS_LN, LN_EPS)), dve(lambda e: e.memset(EPS_RMS, RMS_EPS))]
    xn_tok = []
    G = first_norm()
    for n in range(24):
        next(fill)
        if n > 7:
            next(G, None)
    SKB, C8, LM, QG = SM[:, 36:52], SM[:, 52:56], SM[:, 56:60], SM[:, 60:64]
    v_tok = load_vectors(VECS[3:], "c2")
    for i in range(2):
        bg_tok.append(dma(lambda e, i=i: e.dma_start(
            BG[:, i:i + 1], A["b_gates"][i].rearrange("(a b) -> a b", b=1)), "c3"))
    sk_tok = dma(lambda e: e.dma_start(SK, A["od_sinks_2"]), "c3")

    def late_start():
        for g0 in range(1, ngrp, 4):
            vt_tok.append(turn(g0, min(4, ngrp - g0), v_tok))
        bank, bw = PS.get()
        tok = mm(bank[:, 0:16], CO[0:1, C_ONE:C_ONE + 128], SK, True, True, sk_tok, c_tok, bw, inc=True)
        skb_tok.append(copy("dve", SKB, bank[:, 0:16], tok))
        PS.put(bank, skb_tok[0])
        lam = vec("ev_lam_2", 0, 0, 4)
        t = stt(C8, lam, -1.0, lam, ALU.mult, ALU.min, vt_tok)
        t = af(C8, C8, ACT.Exp, t)
        t = af(C8, C8, ACT.Ln, t, bias=1.0)
        t1 = ts(LM, lam, -1.0, 0.0, ALU.mult, ALU.max, vt_tok)
        t = tt(C8, C8, LM, ALU.add, t, t1)
        c8_tok.append(ts(C8, C8, 8.0, None, ALU.mult, None, t))
        for i, (vn, sc) in enumerate((("ev_qn_g_2", 0.125), ("ev_kn_g_2", 1.0),
                                      ("od_qn_g_2", 0.125), ("od_kn_g_2", 1.0))):
            qg_tok.append(ts(QG[:, i:i + 1], vec(vn, 0, 0, 1), sc, None, ALU.mult, None, vt_tok))

    def taps(q, bank, n, mid, w, b, *wait):
        t = ts(q[:, 0:S], bank[:, :], w(mid), b, ALU.mult, ALU.add, *wait)
        for k in range(n):
            d = k - mid
            if d:
                a, z = max(0, -d), S - max(0, d)
                t = stt(q[:, a:z], bank[:, a + d:z + d], w(k), q[:, a:z], ALU.mult, ALU.add, t)
        PS.put(bank, t)
        return t

    def norm_tiles():
        w = Q.now()
        return ring("nrm", 88, 2, 512, tokens=w), at("nrd", 92, [128, S]), w

    def spread(cols, Dt, lhs, w):
        t = tt(Dt[:, :, :], ident.unsqueeze(1).to_broadcast([128, 4, 128]),
               cols.unsqueeze(2).to_broadcast([128, 4, 128]), ALU.mult, w)
        bank, bw = PS.get()
        tok = mm(bank[:, :], lhs, Dt[:, :, :].rearrange("p a b -> p (a b)"), True, True, t, bw, inc=True)
        return bank, tok

    def rstd(dst, src, scale, eps, w):
        t = af(dst, src, ACT.Sqrt, w, eps_tok, scale=scale, bias=eps)
        return recip(dst, dst, t)

    def warm():
        warm_tok.append(af(WARM, EPS_LN, ACT.Sqrt, eps_tok, warm_tok[-1:]))

    warm_tok = []

    def total(bank, bw, x, i, n, *w):
        return mm(bank[:, :], ones, x, i == 0, i == n - 1, *w, bw, inc=True)

    def norm_ln(htok, mean, g, b, keep, mod):
        sq, R, w0 = norm_tiles()
        pm, tok = mean
        if mod:
            blk, jsc, jsh, part = mod
            ta = [need_ada(blk, p) for p in part]
            ta = ts(S1, ad(blk, jsc), 1.0, None, ALU.add, None, ta, w0)
            tb = tt(B1, S1, b, ALU.mult, ta)
            mt = tt(B1, B1, ad(blk, jsh), ALU.add, tb)
        gt = ts(GB, b, keep, None, ALU.mult, None, w0)
        vb, vw = PS.get()
        for kt in range(NT):
            t = stt(H[:, kt, :], pm[:, :], -1.0 / D, H[:, kt, :], ALU.mult, ALU.add, tok, htok[kt])
            htok[kt] = t
            s, sw = sq.get()
            t = af(s[:, :], H[:, kt, :], ACT.Square, t, sw)
            vt = total(vb, vw, s[:, :], kt, NT, t)
            sq.put(s, vt)
        PS.put(pm, htok[-1])
        tok = rstd(R[:, :], vb[:, :], 1.0 / D, EPS_LN, [vt, w0])
        PS.put(vb, tok)
        if not mod:
            warm()
            sb, sbw = PS.get()
            for kt in range(NT):
                t = stt(H[:, kt, :], H[:, kt, :], g[:, kt:kt + 1], R[:, :], ALU.mult, ALU.mult, tok, htok[kt])
                t = ts(H[:, kt, :], H[:, kt, :], keep, GB[:, kt:kt + 1], ALU.mult, ALU.add, t, gt)
                htok[kt] = [t]
                s, sw = sq.get()
                t = af(s[:, :], H[:, kt, :], ACT.Square, t, sw)
                vt = total(sb, sbw, s[:, :], kt, NT, t)
                sq.put(s, vt)
            return sb, vt
        ut = split_tiles(sq, lambda kt, s, sw: ts(
            s, H[:, kt, :], S1[:, kt:kt + 1], B1[:, kt:kt + 1], ALU.mult, ALU.add,
            stt(H[:, kt, :], H[:, kt, :], g[:, kt:kt + 1], R[:, :], ALU.mult, ALU.mult, tok, htok[kt]),
            mt, sw))
        def scaled(kt):
            htok[kt] = [af(H[:, kt, :], H[:, kt, :], ACT.Identity, ut[kt][0], gt, scale=keep, bias=GB[:, kt:kt + 1])]

        deferred.extend(lambda kt=kt: scaled(kt) for kt in range(NT))
        return ut

    def split_tiles(sq, make):
        ut, back = [], None
        for kt in range(NT + 1):
            if kt < NT:
                s, sw = sq.get()
                t1 = make(kt, s[:, :], sw)
                hi = copy("act", UH[:, kt, :], s[:, :], t1)
            if back:
                k, r, h = back
                lo = tt(UL[:, k, :], r[:, :], UH[:, k, :].bitcast(F32), ALU.subtract, h,
                        eng="pool" if k in (1, 3, 5) else "dve")
                sq.put(r, lo)
                ut.append([h, lo])
            back = (kt, s, hi)
        return ut

    def norm_rms(htok, squares, g, mod):
        sq, R, w0 = norm_tiles()
        blk, jsc, jsh, part = mod
        ta = [need_ada(blk, p) for p in part]
        ta = ts(S1, ad(blk, jsc), 1.0, None, ALU.add, None, ta, w0)
        mt = tt(S1, S1, g, ALU.mult, ta)
        vb, vt = squares
        tok = rstd(R[:, :], vb[:, :], 1.0 / D, EPS_RMS, [vt, w0])
        PS.put(vb, tok)

        def make(kt, s, sw):
            t = tt(s, H[:, kt, :], R[:, :], ALU.mult, tok, sw, htok[kt])
            return ts(s, s, S1[:, kt:kt + 1], ad(blk, jsh, kt, 1), ALU.mult, ALU.add, t, mt)

        return split_tiles(sq, make)

    def residual(name, lay, KT, XH, XL, xtok, htok, gate, sums):
        run_deferred(NT)
        if not callable(sums):
            warm()
        sq = ring("rsq", 88, 2, 512, tokens=Q.now())
        part = at("rsum", 92, [128, S])
        last = NT - 1
        pt_ = Q.now()
        for m in range(NT):
            bank, tok = lin_tile(name, lay, m * 128, KT, XH, XL, xtok)
            if callable(sums) and m:
                sums(m - 1)
            if m == last and sums in ("means", "squares"):
                pm, pw = PS.get()
                total(pm, pw, part[:, :], 0, 2, pt_)
            t = stt(H[:, m, :], bank[:, :], gate[:, m:m + 1], H[:, m, :], ALU.mult, ALU.add, tok, htok[m])
            PS.put(bank, t)
            htok[m] = [t]
            if sums == "squares":
                s, sw = (part, pt_) if m == 0 else sq.get()
                t = af(s[:, :], H[:, m, :], ACT.Square, t, sw)
                if m == 0:
                    pt_ = [t]
                elif m < last:
                    pt_ = [tt(part[:, :], part[:, :], s[:, :], ALU.add, t, pt_)]
                    sq.put(s, pt_)
                else:
                    return pm, total(pm, pw, s[:, :], 1, 2, t)
            elif sums == "means":
                if m == last:
                    return pm, total(pm, pw, H[:, m, :], 1, 2, t)
                if m:
                    a = H[:, 0, :] if m == 1 else part[:, :]
                    pt_ = [tt(part[:, :], a, H[:, m, :], ALU.add, t, pt_)]
        sums(last)

    def turned_back(htok):
        w = Q.now()
        OT = at("OT", 68, [128, 4, D], F32, BASE)
        dst = out[0].rearrange("(b p) d -> p b d", p=128)
        groups = {3: (0, 4), 5: (4, 6), 6: (6, 7), 7: (7, 8)}
        done = []

        def tile(kt):
            bank, bw = PS.get()
            for b in range(4):
                tok = tr(bank[:, b * 128:(b + 1) * 128], H[:, kt, b * 128:(b + 1) * 128], ident, htok[kt], bw,
                         inc=b == 3)
            t = copy("act", OT[:, :, kt * 128:(kt + 1) * 128], bank[:, :].rearrange("p (b f) -> p b f", b=4), tok, w)
            PS.put(bank, t)
            done.append(t)
            if kt in groups:
                c = slice(128 * groups[kt][0], 128 * groups[kt][1])
                out_tok.append(dma(lambda e: e.dma_start(dst[:, :, c], OT[:, :, c]), "out", done))

        return tile

    def roll(tasks, step):
        live = []
        tasks = deque(tasks)
        while tasks or live:
            if tasks:
                live.append(tasks.popleft())
            live = [g for g in live if next(g, live) is not live]
            step(len(tasks))

    def first_attention(lay, ut):
        w0 = Q.now()
        YBH, YBL = at("YBH", 0, [128, 4, S], F32R), at("YBL", 8, [128, 4, S], F32R)
        NUM = at("NUM", 16, [128, 3, 4, S])
        VA = [at(f"VA{i}", 40 + 10 * i, [128, 5, 512]) for i in range(2)]
        vfree = [list(w0), list(w0)]
        qk = ring("qk", 60, 4, 640, tokens=w0)
        sx = ring("sx", 70, 3, 1024, tokens=w0)
        pts = ring("pt", 82, 2, 1024, tokens=w0)
        ND0 = at("ND0", 90, [128, 1024])
        nd_tok = dma(lambda e: e.dma_start(ND0[:, :], A["nd0"]), "c4", w0)
        vtok, made, num_tok = {}, {}, []

        def lins():
            for g in range(3):
                blocks = ([(slice(0, 64), 64)] + [(slice(64 + 128 * i, 192 + 128 * i), 128) for i in range(3)]
                          + [(slice(448, 512), 64)]) if g == 0 else [(slice(q, S, 4), 128) for q in range(4)]
                banks, tok = yield from lin_rows("w_in", lay, 4112 + 3072 + g * 512, blocks, UH, UL, ut)
                if lay == 0 and g == 0:
                    late_start()
                vtok[g] = []
                for i, (bank, (_, m)) in enumerate(zip(banks, blocks)):
                    t = copy(("act", "dve")[i % 2], VA[g % 2][0:m, i, :], bank[0:m, :], tok, vfree[g % 2])
                    PS.put(bank, t)
                    vtok[g].append(t)
                for j in range(4):
                    pair = []
                    for which in range(2):
                        bank, tok = lin_tile("w_in", lay, 4112 + 1536 * which + g * 512 + j * 128, NT, UH, UL, ut)
                        yield
                        q, qw = qk.get()
                        if which and g == 0:
                            z1 = pool(lambda e, q=q: e.memset(q[:, 0:64], 0.0), qw)
                            z2 = pool(lambda e, q=q: e.memset(q[:, 576:640], 0.0), qw)
                            t = copy("act", q[:, 64:576], bank[:, :], tok, qw)
                            PS.put(bank, t)
                            t = [t, z1, z2]
                        else:
                            src = bank[:, :] if g == 0 else bank[:, :].rearrange("p (m r) -> p r m", r=4)
                            dst = q[:, 0:512] if g == 0 else q[:, 0:512].rearrange("p (r m) -> p r m", r=4)
                            t = af(dst, src, ACT.Copy, tok, qw, scale=1.0 if which else 0.125)
                            PS.put(bank, t)
                        pair.append((q, t))
                    made[(g, j)] = pair

        pvs = {}

        def head(g, h):
            j, x = h // 2, h % 2
            while (g, j) not in made:
                next(L, None)
            (q, qt), (k, kt_) = made[(g, j)]
            W = 256 if g == 0 else 128
            V = VA[g % 2]
            po = 64 * x
            banks = [PS.get() for _ in range(2 if g == 0 else 1)]
            for b in range(4):
                bank, bw = banks[b * W // 512]
                c0 = b * W % 512
                tok = mm(bank[:, c0:c0 + W], q[po:po + 64, b * 128:(b + 1) * 128],
                         k[po:po + 64, b * 128:b * 128 + W], True, True, qt, kt_, bw, inc=True)
            if x:
                qk.put(q, tok)
                qk.put(k, tok)
            sc, sw = sx.get()
            for i, (bank, _) in enumerate(banks):
                if g == 0:
                    t = stt(sc[:, 512 * i:512 * i + 512], ND0[:, 512 * i:512 * i + 512], SLOPES[8 * g + h],
                            bank[:, :], ALU.mult, ALU.add, tok, sw, nd_tok)
                else:
                    a = C_ND1 if g == 1 else C_ND2
                    t = stt(sc[:, 0:512].rearrange("p (b w) -> p b w", b=4),
                            CO[:, a:a + 128].unsqueeze(1).to_broadcast([128, 4, 128]), SLOPES[8 * g + h],
                            bank[:, :].rearrange("p (b w) -> p b w", b=4), ALU.mult, ALU.add, tok, sw)
                PS.put(bank, t)
            nm = ST[:, g, 0, :, h]
            t = dve(lambda e: e.tensor_reduce(
                nm, sc[:, 0:4 * W].rearrange("p (b w) -> p b w", b=4), AX.X, ALU.max, negate=True), t, w0)
            for b in range(4):
                te = af(sc[:, b * W:(b + 1) * W], sc[:, b * W:(b + 1) * W], ACT.Exp, t,
                        bias=ST[:, g, 0, b, h:h + 1], accum_out=ST[:, g, 1, b, h:h + 1])
            yield
            p, ptw = pts.get()
            jobs = []
            for b in range(4):
                if g == 0:
                    jobs.append((b, 64, 64, b) if b == 0 else (b, 0, 128, b))
                    jobs.append((b, 128, 64, b + 1) if b == 3 else (b, 128, 128, b + 1))
                else:
                    jobs.append((b, 0, 128, b))
            et = []
            for i0 in range(0, len(jobs), 4):
                bank, bw = PS.get()
                for i in range(i0, i0 + 4):
                    b, c0, m, _ = jobs[i]
                    tok = tr(bank[0:m, (i % 4) * 128:(i % 4 + 1) * 128],
                             sc[:, b * W + c0:b * W + c0 + m], ident, te, bw, inc=True)
                if all(jobs[i][2] == 128 for i in range(i0, i0 + 4)):
                    t = [copy(("act", "dve")[(i0 // 4 + x) % 2], p[:, i0 * 128:(i0 + 4) * 128], bank[:, :],
                              tok, ptw)]
                else:
                    t = []
                    for i in range(i0, i0 + 4):
                        m = jobs[i][2]
                        t.append(copy(("act", "dve")[(i0 // 4 + x) % 2], p[0:m, i * 128:(i + 1) * 128],
                                      bank[0:m, (i % 4) * 128:(i % 4 + 1) * 128], tok, ptw))
                PS.put(bank, *t)
                et += t
            sx.put(sc, tok)
            yield
            if x == 0:
                pvs[0] = PS.get()
            pv, pw = pvs[0]
            for i, (b, c0, m, vb) in enumerate(jobs):
                last = mm(pv[po:po + 64, b * 128:(b + 1) * 128], V[0:m, vb, h * 64:(h + 1) * 64],
                          p[0:m, i * 128:(i + 1) * 128], g > 0 or i % 2 == 0, g > 0 or i % 2 == 1,
                          et, vtok[g], pw, inc=i == len(jobs) - 1)
            pts.put(p, last)
            if x:
                src = pv[:, :] if g == 0 else pv[:, :].rearrange("p (r m) -> p r m", r=4)
                dst = NUM[:, g, j, :] if g == 0 else NUM[:, g, j, :].rearrange("p (m r) -> p r m", r=4)
                t = copy("act", dst, src, last, w0)
                PS.put(pv, t)
                num_tok.append(t)
            if h == 7:
                vfree[g % 2] = [last]

        L = lins()
        while (0, 0) not in made:
            next(L, None)
        late = (2, 3)
        roll([head(g, h) for g in range(3) for h in range(8)],
             lambda left: next(L, None) if late not in made and (left % 2 or len(qk.free)) else filler(1))
        yt = []

        def tail():
            RR = at("RR", 70, [8, 3, 2, S])
            MI = at("MI", 82, [8, 2, S])
            wr = Q.now()
            rt = {}
            for g in range(3):
                for kd in range(2):
                    bank, bw = PS.get()
                    for b in range(4):
                        tok = tr(bank[0:8, b * 128:(b + 1) * 128], ST[:, g, kd, b, :], ident, wr, bw, inc=b == 3)
                    src = bank[0:8, :] if g == 0 else bank[0:8, :].rearrange("p (r m) -> p r m", r=4)
                    dst = RR[:, g, kd, :] if g == 0 else RR[:, g, kd, :].rearrange("p (m r) -> p r m", r=4)
                    t = copy(("act", "dve")[kd], dst, src, tok, wr)
                    PS.put(bank, t)
                    rt[(g, kd)] = t
            yield
            t = tt(MI[:, 0, :], RR[:, 0, 0, :], RR[:, 1, 0, :], ALU.min, rt[(0, 0)], rt[(1, 0)], wr)
            t = tt(MI[:, 0, :], MI[:, 0, :], RR[:, 2, 0, :], ALU.min, rt[(2, 0)], t)
            te = []
            for g in range(3):
                t1 = tt(RR[:, g, 0, :], MI[:, 0, :], RR[:, g, 0, :], ALU.subtract, t)
                te.append(af(RR[:, g, 0, :], RR[:, g, 0, :], ACT.Exp, t1))
            yield
            p = [tt(RR[:, g, 1, :], RR[:, g, 1, :], RR[:, g, 0, :], ALU.mult, te[g], rt[(g, 1)]) for g in range(3)]
            t = tt(MI[:, 1, :], RR[:, 0, 1, :], RR[:, 1, 1, :], ALU.add, p)
            t = tt(MI[:, 1, :], MI[:, 1, :], RR[:, 2, 1, :], ALU.add, t)
            t = recip(MI[:, 1, :], MI[:, 1, :], t)
            wt = [tt(RR[:, g, 0, :], RR[:, g, 0, :], MI[:, 1, :], ALU.mult, t) for g in range(3)]
            yield
            for j in range(4):
                for g in range(3):
                    bank, bw = PS.get()
                    tok = mm(bank[:, :], CO[0:8, C_SEL + 128 * j:C_SEL + 128 * j + 128], RR[:, g, 0, :],
                             True, True, wt[g], bw, inc=True)
                    t = tt(NUM[:, g, j, :], NUM[:, g, j, :], bank[:, :], ALU.mult, tok, num_tok)
                    PS.put(bank, t)
                t = tt(NUM[:, 0, j, :], NUM[:, 0, j, :], NUM[:, 1, j, :], ALU.add, t)
                t = tt(NUM[:, 0, j, :], NUM[:, 0, j, :], NUM[:, 2, j, :], ALU.add, t)
                yt.append(list(hilo(YBH[:, j, :], YBL[:, j, :], NUM[:, 0, j, :], [t, w0])))
                yield
        return YBH, YBL, yt, tail()

    def first_mlstm(lay, ut, tail):
        w0 = Q.now()
        VM = at("VM", 46, [128, 4, D])
        G4 = at("G4", 62, [4, 4, S])
        Z16 = at("Z16", 40, [128, S])
        ONE = at("ONE", 42, [4, S])
        RT = at("RT", 86, [4, 4, S])
        NR = at("NR", 86, [4, 2, S])
        qk_tiles = [at(f"mq{i}", 70 + 2 * i, [128, S]) for i in range(6)]
        vm_tok, sig = [], []
        made = {}
        box = {}

        def gates():
            bank, tok = lin_tile("w_in", lay, 4096, NT, UH, UL, ut)
            t = af(Z16[0:16, :], bank[0:16, :], ACT.Identity, tok, bg_tok, w0, bias=BG[:, lay:lay + 1])
            PS.put(bank, t)
            for j in range(4):
                t1 = dma(lambda e, j=j: e.dma_start(G4[:, j, :], Z16[4 * j:4 * j + 4, :]), "c5", t, w0)
            box["g"] = t1
            yield

        def lins():
            for half in range(2):
                banks, tok = yield from lin_rows("w_in", lay, 2048 + 512 * half,
                                                 [(slice(128 * b, 128 * b + 128), 128) for b in range(4)], UH, UL, ut)
                for b, bank in enumerate(banks):
                    t = copy(("act", "dve")[b % 2], VM[:, b, 512 * half:512 * half + 512], bank[:, :], tok, w0)
                    PS.put(bank, t)
                    vm_tok.append(t)
            box["v"] = 1
            yield
            qk = box["qk"]
            for h in range(4):
                made[h] = []
                for i, f0 in enumerate((2 * h, 2 * h + 1, 8 + 2 * h, 9 + 2 * h)):
                    bank, tok = lin_tile("w_in", lay, f0 * 128, NT, UH, UL, ut)
                    yield
                    q, qw = qk.get()
                    t = taps(q, bank, 5, 2, lambda k, f0=f0: vec("conv_w", lay, 16 * k + f0, 1),
                             vec("conv_b", lay, f0, 1), tok, qw)
                    t = af(q[:, :], q[:, :], ACT.Silu, t)
                    made[h].append((q, t))
            for m in range(6):
                bank, tok = lin_tile("w_in", lay, 3072 + 128 * m, NT, UH, UL, ut)
                yield
                s, sw = qk.get()
                t = af(s[:, :], bank[:, :], ACT.Sigmoid, tok, sw)
                PS.put(bank, t)
                sig.append((s, t))

        def scan(o, a, b, init, op0, op1, *w):
            return dve(lambda e: e.tensor_tensor_scan(o, a, b, init, op0, op1), *w)

        def gate_rows():
            o_t = dve(lambda e: e.memset(ONE[:, :], 1.0), w0)
            F4 = G4[:, 1:4:2, :]
            t = stt(RT[:, 0:2, :], F4, -1.0, F4, ALU.mult, ALU.min, box["g"], w0)
            t = af(RT[:, 0:2, :], RT[:, 0:2, :], ACT.Exp, t)
            t = af(RT[:, 0:2, :], RT[:, 0:2, :], ACT.Ln, t, bias=1.0)
            yield
            t = stt(RT[:, 2:4, :], F4, 0.0, RT[:, 0:2, :], ALU.min, ALU.subtract, t)
            rev = [slice(0, S), slice(S - 1, None, -1)]
            fs = [scan(RT[:, d, rev[d]], ONE[:, :], RT[:, 2 + d, rev[d]], 0.0, ALU.mult, ALU.add, t, o_t)
                  for d in range(2)]
            yield
            at_ = [tt(G4[:, 2 * d, :], G4[:, 2 * d, :], RT[:, d, :], ALU.subtract, fs) for d in range(2)]
            mt = [scan(G4[:, 1 + 2 * d, rev[d]], ONE[:, :], G4[:, 2 * d, rev[d]], NEG, ALU.mult, ALU.max, at_)
                  for d in range(2)]
            yield
            et = stt(RT[:, 0:2, :], RT[:, 0:2, :], -1.0, F4, ALU.mult, ALU.subtract, mt)
            yield
            bank, bw = PS.get()
            for r in range(4):
                src = (G4[:, 0, :], G4[:, 2, :], RT[:, 0, :], RT[:, 1, :])[r]
                for b in range(4):
                    tok = tr(bank[:, 16 * r + 4 * b:16 * r + 4 * b + 4], src[:, b * 128:(b + 1) * 128],
                             CO[0:4, 0:4], et, at_, bw, inc=b == 3)
            t = copy("dve", CL[:, :, :, :].rearrange("p a b c -> p (a b c)"), bank[:, 0:64], tok, w0)
            PS.put(bank, t)
            box["cl"] = t
            box["nt"] = ts(NR[:, :, :], F4, -1.0, None, ALU.mult, None, mt, tok)
            box["em"] = af(EM[:, :, :, :], CL[:, 2:4, :, :], ACT.Exp, t, w0)

        L = lins()
        for _ in gates():
            pass
        GR_ = gate_rows()
        for _ in tail:
            next(L, None)
            next(GR_, None)
        for _ in GR_:
            pass
        w1 = Q.now()
        YA = at("YA", 16, [128, NT, S])
        box.update(qk=Ring(qk_tiles, w1))
        while "v" not in box:
            next(L, None)
        w2 = Q.now()
        PD = [at("PF", 32, [128, 1280]), at("PB", 37, [128, 1280])]
        xr_ = Ring([at(f"xr{i}", 42 + 2 * i, [128, S]) for i in range(2)], w2)
        PX = [at("PX0", 82, [128, 384]), at("PX1", 94, [128, 384])]
        HV = [at(f"HV{i}", 62 + 2 * i, [128, S]) for i in range(2)]
        DT = at("DT", 66, [128, 4, 128])
        NB = [at("NB0", 84, [128, S]), at("NB1", 68, [128, S])]
        SQ = [at("SQ", 66, [128, S]), NB[1]]
        NA = [at(f"NA{i}", 90 + 2 * i, [128, S]) for i in range(2)]
        nt, cl_t, em = box["nt"], box["cl"], box["em"]
        ya_tok = []
        BO = [0, 128, 384, 768]

        rel = {k: w2 for k in ("NA", "PD", "DN", "DT", "NB", "HV", "PX")}

        def part_sums(d, t):
            P, X = PD[d], PX[d]
            a, b = ((128, OFF[1]), (BO[3], BO[2]))[d]
            add = lambda o, x, y, *w: tt(o, x, y, ALU.add, *w, eng="pool")
            t = add(X[:, :], P[:, a:a + 384], P[:, b:b + 384], t, rel["PX"])
            for n, o in ((256, (OFF[2], BO[1])[d]), (128, (OFF[3], BO[0])[d])):
                c = 384 - n if d == 0 else 0
                t = add(X[:, c:c + n], X[:, c:c + n], P[:, o:o + n], t)
            return t

        def head(h):
            while len(made.get(h, ())) < 4:
                next(L, None)
            qk = made[h]
            nt_ = []
            for d in range(2):
                bank, bw = PS.get()
                tok = mm(bank[:, :], CO[0:4, h:h + 1].to_broadcast([4, 128]), NR[:, d, :], True, True,
                         nt, bw, inc=True)
                t = copy("act", NA[d][:, :], bank[:, :], tok, rel["NA"])
                PS.put(bank, t)
                nt_.append(t)
            ptk = [[], []]
            pd_free = rel["PD"]
            for sb in range(4):
                bank, bw = PS.get()
                for kt in range(2):
                    tok = mm(bank[:, :], qk[2 + kt][0][:, sb * 128:(sb + 1) * 128], qk[kt][0][:, :], kt == 0, kt == 1,
                             [x[1] for x in qk], bw, inc=kt == 1)
                for d in range(2):
                    c0, c1 = (sb * 128, 512) if d == 0 else (0, sb * 128 + 128)
                    n = c1 - c0
                    o = (OFF if d == 0 else BO)[sb]
                    x, xw = xr_.get()
                    q0 = 0 if d == 0 else n - 128
                    dg = x[:, q0:q0 + 128]
                    t = ts(dg, NA[d][:, c0 + q0:c0 + q0 + 128], CL[:, d, sb, h:h + 1], 0.0, ALU.add, ALU.min,
                           nt_[d], cl_t, xw)
                    t = te = af(dg, dg, ACT.Exp, t)
                    if n > 128:
                        r0 = 128 - q0 if d == 0 else 0
                        te = af(x[:, r0:r0 + n - 128], NA[d][:, c0 + r0:c0 + r0 + n - 128], ACT.Exp, nt_[d], cl_t, xw,
                                bias=CL[:, d, sb, h:h + 1])
                    sg = 1 if d == 0 else -1
                    t = pool(lambda e, dg=dg, sg=sg: e.affine_select(
                        out=dg, in_=dg, compare_op=ALU.is_ge, fill=0.0, base=0, pattern=[[sg, 128]],
                        channel_multiplier=-sg), t)
                    t = stt(PD[d][:, o:o + n], bank[:, c0:c1], 0.0625, x[:, 0:n], ALU.mult, ALU.mult, tok, t, te, pd_free)
                    xr_.put(x, t)
                    ptk[d].append(t)
                PS.put(bank, ptk[0][-1], ptk[1][-1])
                if sb == 3:
                    for x in qk:
                        box["qk"].put(x[0], tok)
                if sb % 2:
                    yield
            rel["NA"] = ptk
            px = [part_sums(d, ptk[d]) for d in range(2)]
            nb = {}
            for d in range(2):
                for v in range(2):
                    bank, bw = PS.get()
                    sbs = (0, 1, 2, 3) if d == 0 else (3, 2, 1, 0)
                    for i, sb in enumerate(sbs):
                        c0, c1 = (sb * 128, 512) if d == 0 else (0, sb * 128 + 128)
                        o = (OFF if d == 0 else BO)[sb]
                        tok = mm(bank[:, c0:c1], VM[:, sb, h * 256 + v * 128:h * 256 + v * 128 + 128],
                                 PD[d][:, o:o + c1 - c0], i == 0, i == 3, ptk[d], vm_tok, bw, inc=i == 3)
                    nb[(d, v)] = (bank, tok)
                if d:
                    dn, dw = PS.get()
                    for e in range(2):
                        for tb in range(4):
                            whole = tb == (0, 3)[e]
                            o = tb * 128 if e else (tb - 1) * 128
                            src = PD[e][:, (0, BO[3] + 384)[e]:][:, 0:128] if whole else PX[e][:, o:o + 128]
                            tok = mm(dn[:, 4 * e + tb:4 * e + tb + 1], src, onec, True, True, px, ptk, dw, inc=True)
                    rel["PX"] = [tok]
                    rel["PD"] = [tok]
                    t = af(DN, dn[:, 0:8], ACT.Abs, tok, rel["DN"])
                    PS.put(dn, t)
                    t = tt(DN.rearrange("p (d b) -> p d b", d=2), DN.rearrange("p (d b) -> p d b", d=2),
                           EM[:, :, :, h], ALU.max, t, em)
                    rt = recip(DN, DN, t)
                yield
            nt_, tk = [], rel["DT"]
            for d in range(2):
                bk, tk = spread(DN[:, 4 * d:4 * d + 4], DT, ones, [rt, tk])
                t = copy("act", NB[d][:, :], bk[:, :], tk, rel["NB"])
                PS.put(bk, t)
                nt_.append(t)
            rel["DN"] = [tk]
            yield
            hv = []
            for v in range(2):
                b0, t0 = nb[(0, v)]
                b1, t1 = nb[(1, v)]
                x, xw = xr_.get()
                ta = tt(HV[v][:, :], b0[:, :], NB[0][:, :], ALU.mult, t0, nt_, rel["HV"])
                tb_ = tt(x[:, :], b1[:, :], NB[1][:, :], ALU.mult, t1, nt_, xw)
                PS.put(b0, ta)
                PS.put(b1, tb_)
                t = tt(HV[v][:, :], HV[v][:, :], x[:, :], ALU.add, ta, tb_)
                xr_.put(x, t)
                hv.append(t)
            yield
            pm, bw = PS.get()
            for v in range(2):
                tok = total(pm, bw, HV[v][:, :], v, 2, hv[v])
            sqs = []
            for v in range(2):
                t = stt(HV[v][:, :], pm[:, :], -1.0 / 256, HV[v][:, :], ALU.mult, ALU.add, tok)
                sqs.append(af(SQ[v][:, :], HV[v][:, :], ACT.Square, t, tk, hv))
                hv[v] = t
            PS.put(pm, hv[1])
            yield
            bank, bw = PS.get()
            for v in range(2):
                bank_t = total(bank, bw, SQ[v][:, :], v, 2, sqs[v])
            rel["DT"] = [bank_t]
            t = rstd(NB[0][:, :], bank[:, :], 1.0 / 256, EPS_LN, [bank_t, hv])
            PS.put(bank, t)
            for v in range(2):
                t2 = stt(YA[:, 2 * h + v, :], HV[v][:, :], vec("gn_w", lay, 2 * h + v, 1), NB[0][:, :],
                         ALU.mult, ALU.mult, t, w1)
                ya_tok.append(t2)
            rel["HV"] = [t2]
            rel["NB"] = [t2, bank_t]

        tasks = [head(h) for h in range(4)]
        for h in range(5):
            for _ in range(4):
                if h:
                    next(tasks[h - 1], None)
                if h < 4:
                    next(tasks[h])
                if len(box["qk"].free):
                    next(L, None)
        for _ in L:
            pass
        return YA, ya_tok, sig

    def first_block(lay, ut, htok):
        YBH, YBL, ybt, tail = first_attention(lay, ut)
        YA, yat, sig = first_mlstm(lay, ut, tail)
        w0 = Q.now()
        YAH, YAL = at("YAH", 32, [128, NT, S], F32R), at("YAL", 48, [128, NT, S], F32R)
        SH, SL = at("SH", 16, [128, NT, S], F32R), at("SL", 64, [128, NT, S], F32R)
        sg = ring("sg", 82, 6, 512, tokens=w0)
        yt, stk, parts = [], [], {}

        def gate(c0):
            bank, tok = lin_tile("w_in", lay, c0, NT, UH, UL, ut)
            s, sw = sg.get()
            t = af(s[:, :], bank[:, :], ACT.Sigmoid, tok, sw)
            PS.put(bank, t)
            return s, t

        def times(s, t, name, m, KT, XH, XL, xtok):
            bank, tok = lin_tile(name, lay, 128 * m, KT, XH, XL, xtok)
            t = tt(s[:, :], s[:, :], bank[:, :], ALU.mult, t, tok)
            PS.put(bank, t)
            return t

        def branches(m):
            ga = gate(8720 + 128 * m)
            s, t = gate(9744 + 128 * m)
            parts[m] = ga, (s, times(s, t, "w_b", m, 4, YBH, YBL, ybt))

        sig += [gate(3072 + 128 * m) for m in (6, 7)]
        branches(0)
        for m, (s, t) in enumerate(sig):
            t = tt(s[:, :], s[:, :], YA[:, m, :], ALU.mult, t, yat)
            u = hilo(YAH[:, m, :], YAL[:, m, :], s[:, :], [t, w0], eng=("dve", "pool")[m % 2])
            if m > 5:
                sg.put(s, *u)
            yt.append(list(u))
        w1 = Q.now()
        for m in range(NT):
            if m < NT - 1:
                branches(m + 1)
            (s, t), (s2, t2) = parts[m]
            t = times(s, t, "w_a", m, NT, YAH, YAL, yt)
            t = tt(s[:, :], s[:, :], s2[:, :], ALU.add, t, t2)
            sg.put(s2, t)
            u = hilo(SH[:, m, :], SL[:, m, :], s[:, :], [t, w1])
            sg.put(s, *u)
            stk.append(list(u))
        return residual("w_out", lay, NT, SH, SL, stk, htok, ad(lay, 2), "means")

    def ffn(lay, ut, htok, blk, conv):
        w0 = Q.now()
        GH, GL = at("GH", 0, [128, FT, S], F32R), at("GL", 44, [128, FT, S], F32R)
        sg = ring("fg", 88, 3, 512, tokens=w0)
        n1, n2, n3 = ("ffn_w_gate_2", "ffn_w_up_2", "ffn_w_down_2") if conv else ("w1", "w3", "w2")
        gt = []
        for m in range(FT):
            if m == 0:
                (bank, tok), ahead = lin_tiles([(n1, lay, 0), (n2, lay, 0)], NT, UH, UL, ut)
            else:
                bank, tok = lin_tile(n1, lay, 128 * m, NT, UH, UL, ut)
            s, sw = sg.get()
            if conv:
                t = taps(s, bank, 3, 2, lambda k, m=m: vec("ffn_conv_w_2", lay, 22 * k + m, 1),
                         vec("ffn_conv_b_2", lay, m, 1), tok, sw)
                t = af(s[:, 0:512], s[:, 0:512], ACT.Silu, t)
            else:
                t = af(s[:, 0:512], bank[:, :], ACT.Silu, tok, sw)
                PS.put(bank, t)
            bank, tok = lin_tile(n2, lay, 128 * m, NT, UH, UL, ut) if m else ahead
            t = tt(s[:, 0:512], s[:, 0:512], bank[:, :], ALU.mult, t, tok)
            PS.put(bank, t)
            u = hilo(GH[:, m, :], GL[:, m, :], s[:, 0:512], [t, w0], eng=("dve", "pool")[m % 2])
            sg.put(s, *u)
            gt.append(list(u))
        return residual(n3, lay, FT, GH, GL, gt, htok, ad(blk, 5),
                        (turned_back(htok) if lay else "squares") if conv else "means")

    def head_norm(tiles, toks, gcol, tmp, RG, wr):
        bank, bw = PS.get()
        n = len(tiles)
        held = []
        for t_, (x, xt) in enumerate(zip(tiles, toks)):
            s, sw = tmp.get()
            held.append((t_, s, af(s[:, 0:512], x, ACT.Square, xt, sw)))
            if len(held) < 2 and len(tmp.free) and t_ < n - 1:
                continue
            yield
            for i, s, t in held:
                tok = mm(bank[0:8, :], CO[:, C_GI + 8 * i:C_GI + 8 * i + 8], s[:, 0:512], i == 0, i == n - 1,
                         t, bw, inc=True)
                tmp.put(s, tok)
            held = []
        t = rstd(RG[:, :], bank[0:8, :], 1.0, EPS_RMS[0:8, :], [tok, wr])
        PS.put(bank, t)
        yield
        outs = []
        for t_, (x, xt) in enumerate(zip(tiles, toks)):
            bank, bw = PS.get()
            tok = mm(bank[:, :], CO[0:8, C_SEL + 128 * t_:C_SEL + 128 * t_ + 128], RG[:, :], True, True, t, bw,
                     inc=True)
            t2 = stt(x, x, gcol, bank[:, :], ALU.mult, ALU.mult, tok, xt, qg_tok)
            PS.put(bank, t2)
            outs.append(t2)
        return outs

    def even_layer(ut, htok):
        w0 = Q.now()
        YH, YL = at("YH", 0, [128, NT, S], F32R), at("YL", 16, [128, NT, S], F32R)
        XR, GR = at("XR", 32, [128, 4, S]), at("GR", 40, [128, 4, S])
        QK = at("QK", 48, [128, 8, S])
        V = at("V", 64, [128, 4, 512])
        BD = at("BD", 72, [128, 2, 4, 128])
        RG = [at(f"RG{i}", 76 + 2 * i, [8, S]) for i in range(2)]
        tmp = ring("etmp", 82.125, 6, 512, tokens=w0)
        t = pool(lambda e: e.memset(BD[:, :, :, :], 0.0), w0)
        for a, wn in enumerate(("ev_wa_2", "ev_wx_2")):
            for par in range(2):
                src = A[wn][0].rearrange("(t x) k j -> x k t j", x=2)[par]
                bd_tok = dma(lambda e, a=a, par=par, src=src: e.dma_start(
                    BD[64 * par:64 * par + 64, a, :, 64 * par:64 * par + 64], src), "c6", t)
        yt = [None] * 8
        vt, nqk = [], []

        def lins():
            qt = []
            two = lin_tiles([("ev_w_in_2", 0, 1024), ("ev_w_in_2", 0, 1152)], NT, UH, UL, ut)
            for i in range(8):
                bank, tok = two[i] if i < 2 else lin_tile("ev_w_in_2", 0, 1024 + 128 * i, NT, UH, UL, ut)
                yield
                t = copy("act", QK[:, i, :], bank[:, :], tok, w0)
                PS.put(bank, t)
                qt.append(t)
            G = lin_rows("ev_w_in_2", 0, 2048, [(slice(128 * b, 128 * b + 128), 128) for b in range(4)], UH, UL, ut)
            next(G)
            yield
            N = head_norms(qt)
            for n in range(7):
                next(N, None)
                if n in (2, 5):
                    next(G)
                yield
            banks, tok = yield from G
            for b, bank in enumerate(banks):
                t = copy(("act", "dve")[b % 2], V[:, b, :], bank[:, :], tok, w0)
                PS.put(bank, t)
                vt.append(t)

        def head_norms(qt):
            for a in range(2):
                r = yield from head_norm([QK[:, 4 * a + i, :] for i in range(4)], qt[4 * a:4 * a + 4],
                                         QG[:, a:a + 1], tmp, RG[a], w0)
                nqk.append(r)

        def lru():
            for i in range(4):
                bank, tok = lin_tile("ev_w_in_2", 0, 128 * i, NT, UH, UL, ut)
                yield
                t = taps(XR[:, i, :], bank, 4, 3, lambda k, i=i: vec("ev_conv_w_2", 0, 4 * k + i, 1),
                         vec("ev_conv_b_2", 0, i, 1), tok, w0)
                bank, tok = lin_tile("ev_w_in_2", 0, 512 + 128 * i, NT, UH, UL, ut)
                yield
                g_t = af(GR[:, i, :], bank[:, :], ACT.Gelu_apprx_tanh, tok, w0)
                PS.put(bank, g_t)
                g = []
                for a, bn in enumerate(("ev_ba_2", "ev_bx_2")):
                    bank, bw = PS.get()
                    tok = mm(bank[:, :], BD[:, a, i, :], XR[:, i, :], True, True, t, bd_tok, bw, inc=True)
                    s, sw = tmp.get()
                    t1 = af(s[:, :], bank[:, :], ACT.Sigmoid, tok, sw, bias=vec(bn, 0, i, 1))
                    PS.put(bank, t1)
                    g.append((s, t1))
                yield
                (r, rt), (ii, it) = g
                it = tt(ii[:, :], ii[:, :], XR[:, i, :], ALU.mult, it)
                rt = ts(r[:, :], r[:, :], C8[:, i:i + 1], None, ALU.mult, None, rt, c8_tok)
                th, thw = tmp.get()
                ac, acw = tmp.get()
                t1 = af(th[:, :], r[:, :], ACT.Tanh, rt, thw)
                t2 = af(ac[:, :], r[:, :], ACT.Exp, rt, acw, scale=-1.0)
                t3 = ts(r[:, :], th[:, :], 1.0, None, ALU.add, None, t1, t2)
                t3 = recip(r[:, :], r[:, :], t3)
                t3 = stt(r[:, :], th[:, :], 2.0, r[:, :], ALU.mult, ALU.mult, t3)
                t3 = af(r[:, :], r[:, :], ACT.Sqrt, t3)
                yield
                t3 = tt(ii[:, :], ii[:, :], r[:, :], ALU.mult, t3, it)
                t3 = dve(lambda e, th=th, ac=ac, ii=ii: e.tensor_tensor_scan(
                    th[:, :], ac[:, :], ii[:, :], 0.0, ALU.mult, ALU.add), t3, t2)
                t3 = tt(th[:, :], th[:, :], GR[:, i, :], ALU.mult, t3, g_t)
                u = hilo(YH[:, i, :], YL[:, i, :], th[:, :], [t3, w0])
                yt[i] = list(u)
                for x in (r, ii, ac):
                    tmp.put(x, t3)
                tmp.put(th, *u)

        L, R = lins(), lru()
        while next(L, L) is not L:
            next(R, None)
        for _ in R:
            pass
        nq, nk = nqk
        w1 = Q.now()
        zr = Ring([at(f"zs{i}", (32, 37, 42, 72)[i], [128, 1280]) for i in range(4)], w1)
        spr = Ring([at(f"sp{i}", 77 + 5 * i, [128, 1280]) for i in range(3)], w1)
        box = {}

        def head(h):
            i, po = h // 2, 64 * (h % 2)
            z, zw = zr.get()
            sp, spw = spr.get()
            zt = []
            for kb in range(4):
                n = 512 - 128 * kb
                o = OFF[kb]
                bank, bw = PS.get()
                tok = mm(bank[:, 0:n], QK[po:po + 64, 4 + i, kb * 128:(kb + 1) * 128],
                         QK[po:po + 64, i, kb * 128:512], True, True, nq, nk, bw, inc=True)
                t = copy("dve", z[:, o:o + n], bank[:, 0:n], tok, zw)
                PS.put(bank, t)
                dg = z[:, o:o + 128]
                zt.append(pool(lambda e, dg=dg: e.affine_select(
                    out=dg, in_=dg, compare_op=ALU.is_gt, fill=NEG, base=0, pattern=[[1, 128]],
                    channel_multiplier=-1), t))
            t = stt(sp[:, :], z[:, :], -1.0, z[:, :], ALU.mult, ALU.min, zt, spw)
            t = af(sp[:, :], sp[:, :], ACT.Exp, t)
            t = af(sp[:, :], sp[:, :], ACT.Ln, t, bias=1.0)
            yield
            t = stt(sp[:, :], z[:, :], 0.0, sp[:, :], ALU.max, ALU.add, t)
            yield
            wt = []
            for kb in range(4):
                n = 512 - 128 * kb
                o = OFF[kb]
                bank, bw = PS.get()
                for k2 in range(kb, 4):
                    tok = mm(bank[:, 128 * (k2 - kb):n], tri if k2 == kb else ones, sp[:, OFF[k2]:OFF[k2 + 1]],
                             k2 == kb, k2 == 3, t, bw, inc=k2 == 3)
                t1 = tt(z[:, o:o + n], z[:, o:o + n], bank[:, 0:n], ALU.subtract, tok)
                PS.put(bank, t1)
                wt.append(af(z[:, o:o + n], z[:, o:o + n], ACT.Exp, t1))
            spr.put(sp, tok)
            yield
            if h % 2 == 0:
                box["pv"] = PS.get()
            pv, pw = box["pv"]
            for kb in range(4):
                tok = mm(pv[po:po + 64, 128 * kb:512], V[:, kb, h * 64:(h + 1) * 64], z[:, OFF[kb]:OFF[kb + 1]],
                         kb == 0, kb == 3, wt[kb], vt, pw, inc=kb == 3)
            zr.put(z, tok)
            if h % 2:
                hi = copy("act", YH[:, 4 + i, :], pv[:, :], tok)
                yield
                lo = tt(YL[:, 4 + i, :], pv[:, :], YH[:, 4 + i, :].bitcast(F32), ALU.subtract, hi)
                PS.put(pv, lo)
                yt[4 + i] = [hi, lo]

        hs = [head(h) for h in range(8)]
        next(hs[0])
        next(hs[1])
        next(hs[0])
        for h in range(8):
            next(hs[h])
            if h < 7:
                next(hs[h + 1])
            if h < 6:
                next(hs[h + 2])
            if h:
                next(hs[h - 1], None)
            next(hs[h], None)
        next(hs[7], None)
        return residual("ev_w_out_2", 0, NT, YH, YL, yt, htok, ad(2, 2), "squares")

    def odd_layer(ut, htok):
        w0 = Q.now()
        YH, YL = at("OYH", 0, [128, NT, S], F32R), at("OYL", 16, [128, NT, S], F32R)
        QT = at("QT", 32, [128, NT, S])
        KT_ = at("KT", 48, [128, 2, 640])
        V = at("OV", 53, [128, 4, 256])
        MK = at("MK", 57, [128, 1024])
        KD = at("KD", 61, [128, 4, 640])
        sx = ring("ox", 71, 3, 1024, tokens=w0)
        pts = ring("op", 83, 2, 1024, tokens=w0)
        RG = at("ORG", 91, [8, S])
        tmp = ring("otmp", 93, 1, 512, tokens=w0)
        mk_tok = dma(lambda e: e.dma_start(MK[:, :], A["swa"]), "c7", w0)
        kt, vt, qt, kd, yt = [], [], {}, [], []

        def lins():
            two = lin_tiles([("od_w_in_2", 0, 1024), ("od_w_in_2", 0, 1152)], NT, UH, UL, ut)
            for i, (bank, tok) in enumerate(two):
                z = pool(lambda e, i=i: e.memset(KT_[:, i, 0:128], 0.0), w0)
                t = copy("act", KT_[:, i, 128:640], bank[:, :], tok, w0)
                PS.put(bank, t)
                kt.append([t, z])
            kn = head_norm([KT_[:, i, 128:640] for i in range(2)], kt, QG[:, 3:4], tmp, RG, w0)
            next(kn)
            cs = [weights((True, "od_w_in_2", 0, 4 * i, 4, 1280, 256)) for i in range(2)]
            for b in range(4):
                bank, bw = PS.get()
                for k in range(NT):
                    c, q = cs[k // 4], k % 4
                    xs = slice(128 * b, 128 * b + 128)
                    wh, wl = (c[y][:, q * 256:(q + 1) * 256] for y in ("hi", "lo"))
                    mm(bank[:, 0:256], UH[:, k, xs], wh, k == 0, False, c["w1"], ut[k], bw)
                    mm(bank[:, 0:256], UH[:, k, xs], wl, False, False, c["w2"])
                    tok = mm(bank[:, 0:256], UL[:, k, xs], wh, False, k == 7, inc=k == 7)
                t = copy(("act", "dve")[b % 2], V[:, b, :], bank[:, 0:256], tok, w0)
                PS.put(bank, t)
                vt.append(t)
                if b < 2:
                    next(kn)
            for c in cs:
                weights_done(c, tok)
            nk = yield from kn
            for kv in range(4):
                for x in range(2):
                    p0 = 64 * (kv % 2)
                    t = dma(lambda e, kv=kv, x=x, p0=p0: e.dma_start(
                        KD[64 * x:64 * x + 64, kv, :], KT_[p0:p0 + 64, kv // 2, :]), "c8", nk, kt, w0)
            kd.append(t)
            norms = deque()
            both = Ring([tmp.free[0][0], at("otm2", 48, [128, S])], [tmp.free[0][1], t])
            for i in range(16):
                if i < 8:
                    bank, tok = lin_tile("od_w_in_2", 0, 128 * i, NT, UH, UL, ut)
                if norms and next(norms[0], norms) is norms:
                    norms.popleft()
                yield
                if i < 8:
                    t = copy("act", QT[:, i, :], bank[:, :], tok, w0)
                    PS.put(bank, t)
                    qt[("raw", i)] = t
                if i % 4 == 3 and i < 8:
                    norms.append(q_norm(i // 4, both, nk))

        def q_norm(g, tmp, nk):
            idx = range(4 * g, 4 * g + 4)
            outs = yield from head_norm([QT[:, i, :] for i in idx], [qt[("raw", i)] for i in idx], QG[:, 2:3],
                                        tmp, RG, nk if g == 0 else qt[3])
            for i in idx:
                qt[i] = outs[i - 4 * g]

        small = Ring([tuple(SM[:, a + 4 * i:a + 4 * i + 4] for i in range(3)) for a in (112, 136, 148)], w0)
        pvs = {}

        def head(h):
            i, x = h // 2, h % 2
            kv, po = i // 2, 64 * x
            while i not in qt:
                next(L, None)
            banks = [PS.get() for _ in range(2)]
            for b in range(4):
                bank, bw = banks[b // 2]
                c0 = 256 * (b % 2)
                tok = mm(bank[:, c0:c0 + 256], QT[po:po + 64, i, b * 128:(b + 1) * 128],
                         KD[po:po + 64, kv, b * 128:b * 128 + 256], True, True, qt[i], kd[0], bw, inc=True)
            sc, sw = sx.get()
            for n, (bank, _) in enumerate(banks):
                t = tt(sc[:, 512 * n:512 * n + 512], bank[:, :], MK[:, 512 * n:512 * n + 512], ALU.add,
                       tok, sw, mk_tok)
                PS.put(bank, t)
            sm, wm = small.get()
            mx, ex, dn = sm
            t = dve(lambda e: e.tensor_reduce(mx, sc[:, :].rearrange("p (b w) -> p b w", b=4), AX.X, ALU.max), t, wm)
            t = ts(mx, mx, SKB[:, h:h + 1], -1.0, ALU.max, ALU.mult, t, skb_tok)
            t0 = af(ex, mx, ACT.Exp, t, wm, bias=SKB[:, h:h + 1])
            for b in range(4):
                te = af(sc[:, b * 256:(b + 1) * 256], sc[:, b * 256:(b + 1) * 256], ACT.Exp, t,
                        bias=mx[:, b:b + 1], accum_out=dn[:, b:b + 1])
            yield
            t = tt(dn, dn, ex, ALU.add, te, t0)
            t = recip(dn, dn, t)
            tn = []
            for b in range(4):
                tn.append(ts(sc[:, b * 256:(b + 1) * 256], sc[:, b * 256:(b + 1) * 256], dn[:, b:b + 1], None,
                             ALU.mult, None, t))
            small.put(sm, tn)
            yield
            p, ptw = pts.get()
            et = []
            for half in range(2):
                bank, bw = PS.get()
                lo_ = 1 if half == 0 else 0
                for n in range(lo_, 4):
                    c0 = 512 * half + 128 * n
                    tok = tr(bank[:, n * 128:(n + 1) * 128], sc[:, c0:c0 + 128], ident, tn[c0 // 256], bw, inc=n == 3)
                t = copy("dve", p[:, 512 * half + 128 * lo_:512 * half + 512],
                         bank[:, 128 * lo_:512], tok, ptw)
                PS.put(bank, t)
                et.append(t)
            sx.put(sc, tok)
            yield
            if x == 0:
                pvs[0] = PS.get()
            pv, pw = pvs[0]
            for b in range(4):
                for n in range(2):
                    if b == 0 and n == 0:
                        continue
                    last = mm(pv[po:po + 64, b * 128:(b + 1) * 128], V[:, b - 1 + n, kv * 64:(kv + 1) * 64],
                              p[:, 256 * b + 128 * n:256 * b + 128 * n + 128], n == 0 or b == 0, n == 1,
                              et, vt, pw, inc=b == 3 and n == 1)
            pts.put(p, last)
            if x:
                hi = copy("act", YH[:, i, :], pv[:, :], last, w0)
                yield
                lo = tt(YL[:, i, :], pv[:, :], YH[:, i, :].bitcast(F32), ALU.subtract, hi, last, w0)
                PS.put(pv, lo)
                yt.append([hi, lo])

        L = lins()
        roll([head(h) for h in range(16)], lambda left: next(L, None))
        return residual("od_w_out_2", 0, NT, YH, YL, yt, htok, ad(3, 2), "squares")

    out_tok = []
    w0 = Q.now()
    sq, _, _ = norm_tiles()
    ta = [need_ada(0, 0)]
    ta = ts(S1, ad(0, 1), 1.0, None, ALU.add, None, ta)
    ut, htok = [], []
    for kt in range(NT):
        bank, bw = PS.get()
        for b in range(4):
            tok = tr(bank[:, b * 128:(b + 1) * 128], X0[:, b, kt * 128:(kt + 1) * 128], ident, xn_tok, bw, inc=b == 3)
        s, sw = sq.get()
        t1 = ts(s[:, :], bank[:, :], S1[:, kt:kt + 1], ad(0, 0, kt, 1), ALU.mult, ALU.add, tok, ta, sw)
        ha = af(H[:, kt, :], bank[:, :], ACT.Copy, tok, t1, scale=ALPHA)
        PS.put(bank, t1, ha)
        htok.append([ha])
        u = list(hilo(UH[:, kt, :], UL[:, kt, :], s[:, :], t1))
        sq.put(s, *u)
        ut.append(u)
    for lay in range(2):
        mean = first_block(lay, ut, htok)
        ut = norm_ln(htok, mean, vec("ln1_g", lay, 0, 8), vec("ln1_b", lay, 0, 8), ALPHA, (lay, 4, 3, (1, 2)))
        mean = ffn(lay, ut, htok, lay, False)
        if lay == 0:
            ut = norm_ln(htok, mean, vec("ln2_g", 0, 0, 8), vec("ln2_b", 0, 0, 8), ALPHA, (1, 1, 0, (0,)))
        else:
            squares = norm_ln(htok, mean, vec("ln2_g", 1, 0, 8), vec("ln2_b", 1, 0, 8), 1.0, None)
    for lay in range(2):
        ut = norm_rms(htok, squares, vec("norm_mix_g_2", lay, 0, 8), (2 + lay, 1, 0, (0, 1)))
        squares = (even_layer, odd_layer)[lay](ut, htok)
        ut = norm_rms(htok, squares, vec("norm_ffn_g_2", lay, 0, 8), (2 + lay, 4, 3, (1, 2)))
        squares = ffn(lay, ut, htok, 2 + lay, True)
    Q.wait("sp", out_tok)
    if dry:
        return used
    assert st["get"] == len(order)
    emit(nc, Q)


def emit(nc, Q):
    with ExitStack() as ctx:
        sems = {s: ctx.enter_context(nc.semaphore(f"s_{s}")) for s in Q.count}
        block = ctx.enter_context(nc.Block())

        def run(eng, queue):
            for s, n, fn in queue:
                if fn is None:
                    eng.wait_ge(sems[s], n)
                elif n:
                    fn(eng).then_inc(sems[s], n)
                else:
                    fn(eng)

        @block.tensor
        def _(e):
            run(e, Q.q["pe"])

        @block.scalar
        def _(e):
            run(e, Q.q["act"])

        @block.vector
        def _(e):
            run(e, Q.q["dve"])

        @block.gpsimd
        def _(e):
            run(e, Q.q["pool"])

        @block.sync
        def _(e):
            run(e, Q.q["sp"])


_INS = ["x", "c", "w_in", "b_gates", "conv_w", "conv_b", "gn_w", "w_a", "w_b", "w_out", "w_ada", "b_ada",
        "ln1_g", "ln1_b", "w1", "w3", "w2", "ln2_g", "ln2_b", "c_2", "ada_w_2", "ada_b_2", "norm_mix_g_2",
        "norm_ffn_g_2", "ev_w_in_2", "ev_conv_w_2", "ev_conv_b_2", "ev_wa_2", "ev_ba_2", "ev_wx_2", "ev_bx_2",
        "ev_lam_2", "ev_qn_g_2", "ev_kn_g_2", "ev_w_out_2", "od_w_in_2", "od_qn_g_2", "od_kn_g_2", "od_sinks_2",
        "od_w_out_2", "ffn_w_gate_2", "ffn_w_up_2", "ffn_conv_w_2", "ffn_conv_b_2", "ffn_w_down_2"]


def kernel(**inputs):
    import numpy as _np
    import concourse.bacc as _bacc
    from concourse import mybir as _mybir
    from concourse.bass_utils import run_bass_kernel_spmd as _run

    nc = _bacc.Bacc("TRN2", target_bir_lowering=False, num_devices=1)
    arrays, A = {}, {}
    consts = dict(zip(("const", "nd0", "swa"), shape_constants()))
    for name in _INS + list(consts):
        a = consts[name] if name in consts else _np.ascontiguousarray(inputs[name])
        arrays[f"in_{name}"] = a
        A[name] = nc.dram_tensor(f"in_{name}", a.shape, _mybir.dt.from_np(a.dtype), kind="ExternalInput").ap()
    out = nc.dram_tensor("out_0", (1, S, D), _mybir.dt.float32, kind="ExternalOutput").ap()
    order = program(None, A, out, None)
    program(nc, A, out, order)
    r = _run(nc, [arrays], core_ids=[0])
    return r.results[0]["out_0"]
```
